# Optimizing a Trainium2 kernel written in Bass

```python
import math
import jax, jax.numpy as jnp
from jax import lax
import numpy as np

D_MODEL = 1024
BATCH = 1
SEQ = 1024
DEPTH = 2
DEC_BATCH = 1
DEC_SEQ = 64
PAST_LEN = 256

CHUNK = 64
QUERY_BLOCK = 128
N_EVEN = (DEPTH + 1) // 2
N_ODD = DEPTH // 2
MLA_HEADS = 8
Q_RANK = 384
KV_RANK = 256
NOPE_DIM = 64
ROPE_DIM = 32
V_DIM = 64
ROPE_THETA = 10000.0
MLA_WIDTH = MLA_HEADS * V_DIM
SC_WIDTH = 512
SC_K = 3
MIX_E = MLA_WIDTH + SC_WIDTH
DN_HEADS = 8
DN_DK = 128
DN_DV = 128
DN_CONV = 4
DN_KEY = DN_HEADS * DN_DK
DN_VAL = DN_HEADS * DN_DV
DN_QKV = 2 * DN_KEY + DN_VAL
D_FF = 2816
FF_K = 3
EVEN_IN = Q_RANK + KV_RANK + ROPE_DIM + 3 * SC_WIDTH
E_SPLITS = (Q_RANK, Q_RANK + KV_RANK, Q_RANK + KV_RANK + ROPE_DIM,
            Q_RANK + KV_RANK + ROPE_DIM + SC_WIDTH, Q_RANK + KV_RANK + ROPE_DIM + 2 * SC_WIDTH)
ODD_IN = DN_QKV + DN_VAL + 2 * DN_HEADS
O_SPLITS = (DN_QKV, DN_QKV + DN_VAL, DN_QKV + DN_VAL + DN_HEADS)
ALPHA = (2 * DEPTH) ** 0.25
BETA_INIT = (8 * DEPTH) ** -0.25
NORM_EPS = 1e-6
NEG_INF = -1e30

kernel_name = "hybrid_mla_shortconv_gdn_convffn_stream_step"

def layer_norm(x, g, b):
    xf = x.astype(jnp.float32)
    mu = xf.mean(-1, keepdims=True)
    var = jnp.square(xf - mu).mean(-1, keepdims=True)
    return ((xf - mu) * lax.rsqrt(var + NORM_EPS) * g + b).astype(x.dtype)

def rms_norm(x, g):
    xf = x.astype(jnp.float32)
    return (xf * lax.rsqrt(jnp.mean(xf * xf, -1, keepdims=True) + NORM_EPS) * g).astype(x.dtype)

def l2_norm(x):
    xf = x.astype(jnp.float32)
    return xf * lax.rsqrt(jnp.sum(xf * xf, -1, keepdims=True) + NORM_EPS)

def causal_dwconv(x, w, buf):
    k = w.shape[0]
    s = x.shape[1]
    xp = jnp.concatenate([buf.astype(x.dtype), x], axis=1)
    y = xp[:, 0:s] * w[0]
    for i in range(1, k):
        y = y + xp[:, i:i + s] * w[i]
    return y, xp[:, xp.shape[1] - (k - 1):]

def rope(x, pos):
    half = ROPE_DIM // 2
    inv = ROPE_THETA ** (-jnp.arange(half, dtype=jnp.float32) / half)
    ang = pos.astype(jnp.float32)[:, None] * inv[None, :]
    cos = jnp.cos(ang)[None, :, None, :]
    sin = jnp.sin(ang)[None, :, None, :]
    xf = x.astype(jnp.float32)
    x1, x2 = xf[..., :half], xf[..., half:]
    return jnp.concatenate([x1 * cos - x2 * sin, x2 * cos + x1 * sin], -1).astype(x.dtype)

def chunk_attention(q, k, v, q_pos, k_pos):
    b, sq, h, dqk = q.shape
    dv = v.shape[-1]
    qb = QUERY_BLOCK if sq % QUERY_BLOCK == 0 else sq
    nb = sq // qb
    q_blocks = jnp.moveaxis(q.reshape(b, nb, qb, h, dqk), 1, 0)
    pos_blocks = q_pos.reshape(nb, qb)
    k_chunk = k_pos // CHUNK
    scale = (NOPE_DIM + ROPE_DIM) ** -0.5

    def one_block(args):
        qi, pi = args
        s = jnp.einsum('bqhd,bkhd->bhqk', qi, k).astype(jnp.float32) * scale
        visible = k_chunk[None, :] <= (pi // CHUNK)[:, None]
        s = jnp.where(visible[None, None], s, NEG_INF)
        p = jax.nn.softmax(s, axis=-1).astype(v.dtype)
        return jnp.einsum('bhqk,bkhd->bqhd', p, v)

    o = lax.map(one_block, (q_blocks, pos_blocks))
    return jnp.moveaxis(o, 0, 1).reshape(b, sq, h * dv)

def even_mixer(x, q_pos, k_pos, past_lat, past_kr, sc_buf, w_in, g_q, g_kv, w_uq, w_ukv, sc_w, w_o):
    b, s, _ = x.shape
    h = x @ w_in
    c_q, c_kv, k_r, gate_b, gate_c, sh = jnp.split(h, list(E_SPLITS), axis=-1)
    q = (rms_norm(c_q, g_q) @ w_uq).reshape(b, s, MLA_HEADS, NOPE_DIM + ROPE_DIM)
    q = jnp.concatenate([q[..., :NOPE_DIM], rope(q[..., NOPE_DIM:], q_pos)], -1)
    lat = rms_norm(c_kv, g_kv)
    kr = rope(k_r[:, :, None, :], q_pos)[:, :, 0]
    lat_all = jnp.concatenate([past_lat.astype(x.dtype), lat], 1)
    kr_all = jnp.concatenate([past_kr.astype(x.dtype), kr], 1)
    t = lat_all.shape[1]
    kv = (lat_all @ w_ukv).reshape(b, t, MLA_HEADS, NOPE_DIM + V_DIM)
    k = jnp.concatenate([kv[..., :NOPE_DIM],
                         jnp.broadcast_to(kr_all[:, :, None, :], (b, t, MLA_HEADS, ROPE_DIM))], -1)
    v = kv[..., NOPE_DIM:]
    o_att = chunk_attention(q, k, v, q_pos, k_pos)
    u, sc_new = causal_dwconv(gate_c * sh, sc_w, sc_buf)
    o_sc = gate_b * u
    y = jnp.concatenate([o_att, o_sc], -1) @ w_o
    return y, lat, kr, sc_new

def gated_delta_chunked(q, k, v, g, beta, s0):
    f32 = jnp.float32
    b, s, h, dk = q.shape
    dv = v.shape[-1]
    L = CHUNK if s % CHUNK == 0 else s
    n = s // L

    def blk(t):
        t = t.astype(f32).reshape((b, n, L, h) + t.shape[3:])
        return jnp.moveaxis(t, 3, 1)

    q, k, v, g, beta = blk(q), blk(k), blk(v), blk(g), blk(beta)
    G = jnp.cumsum(g, axis=-1)
    tri = jnp.tril(jnp.ones((L, L), bool))
    strict = jnp.tril(jnp.ones((L, L), bool), -1)
    decay = jnp.exp(jnp.where(tri, G[..., :, None] - G[..., None, :], -jnp.inf))
    kb = k * beta[..., None]
    m = jnp.where(strict, jnp.einsum('bhnid,bhnjd->bhnij', kb, k) * decay, 0.0)
    a = m + jnp.eye(L, dtype=f32)
    rhs = jnp.concatenate([v * beta[..., None], kb * jnp.exp(G)[..., None]], -1)
    sol = lax.linalg.triangular_solve(a, rhs, left_side=True, lower=True, unit_diagonal=True)
    w_val, k_cd = sol[..., :dv], sol[..., dv:]
    attn = jnp.einsum('bhnid,bhnjd->bhnij', q, k) * decay
    q_dec = q * jnp.exp(G)[..., None]
    g_last = G[..., -1:]
    k_tail = k * jnp.exp(g_last - G)[..., None]
    g_tot = jnp.exp(g_last[..., 0])

    def step(st, inp):
        qd, kcd, wv, at, kt, gt = inp
        v_new = wv - jnp.einsum('bhld,bhde->bhle', kcd, st)
        o = jnp.einsum('bhld,bhde->bhle', qd, st) + jnp.einsum('bhij,bhje->bhie', at, v_new)
        st = st * gt[..., None, None] + jnp.einsum('bhld,bhle->bhde', kt, v_new)
        return st, o

    xs = tuple(jnp.moveaxis(t, 2, 0) for t in (q_dec, k_cd, w_val, attn, k_tail, g_tot))
    s_fin, o = lax.scan(step, s0.astype(f32), xs)
    o = jnp.moveaxis(jnp.moveaxis(o, 0, 2), 1, 3).reshape(b, s, h, dv)
    return o, s_fin

def odd_mixer(x, dconv_buf, s0, w_in, dconv_w, a_log, dt_bias, g_o, w_o):
    b, s, _ = x.shape
    h = x @ w_in
    qkv, z, a, bt = jnp.split(h, list(O_SPLITS), axis=-1)
    qkv, dconv_new = causal_dwconv(qkv, dconv_w, dconv_buf)
    qkv = jax.nn.silu(qkv)
    q, k, v = jnp.split(qkv, [DN_KEY, 2 * DN_KEY], axis=-1)
    q = l2_norm(q.reshape(b, s, DN_HEADS, DN_DK)) * (DN_DK ** -0.5)
    k = l2_norm(k.reshape(b, s, DN_HEADS, DN_DK))
    v = v.reshape(b, s, DN_HEADS, DN_DV)
    beta = jax.nn.sigmoid(bt.astype(jnp.float32))
    g = -jnp.exp(a_log.astype(jnp.float32)) * jax.nn.softplus(a.astype(jnp.float32) + dt_bias)
    o, s_new = gated_delta_chunked(q, k, v, g, beta, s0)
    o = rms_norm(o, g_o) * jax.nn.silu(z.reshape(b, s, DN_HEADS, DN_DV).astype(jnp.float32))
    y = o.astype(x.dtype).reshape(b, s, DN_VAL) @ w_o
    return y, dconv_new, s_new.astype(s0.dtype)

def conv_ffn(x, buf, w_in, conv_w, w_out):
    h = x @ w_in
    gate, up = h[..., :D_FF], h[..., D_FF:]
    gate, buf_new = causal_dwconv(gate, conv_w, buf)
    return (jax.nn.silu(gate) * up) @ w_out, buf_new

def trunk(x, past_lat, past_kr, sc_buf, dconv_buf, delta_s, ff_buf, w):
    (w_in_e, g_qnorm, g_kvnorm, w_uq, w_ukv, sc_w, w_o_e, w_in_o, dconv_w, a_log, dt_bias,
     g_onorm, w_o_o, w_ff_in, ffconv_w, w_ff_out, ln_mix_g, ln_mix_b, ln_ff_g, ln_ff_b) = w
    s = x.shape[1]
    p = past_lat.shape[2]
    q_pos = p + jnp.arange(s, dtype=jnp.int32)
    k_pos = jnp.arange(p + s, dtype=jnp.int32)
    lats, krs, scs, dcs, dss, ffs = [], [], [], [], [], []
    for i in range(DEPTH):
        if i % 2 == 0:
            e = i // 2
            y, lat, kr, scb = even_mixer(x, q_pos, k_pos, past_lat[e], past_kr[e], sc_buf[e],
                                         w_in_e[e], g_qnorm[e], g_kvnorm[e], w_uq[e], w_ukv[e],
                                         sc_w[e], w_o_e[e])
            lats.append(lat); krs.append(kr); scs.append(scb)
        else:
            o = i // 2
            y, dcb, st = odd_mixer(x, dconv_buf[o], delta_s[o], w_in_o[o], dconv_w[o], a_log[o],
                                   dt_bias[o], g_onorm[o], w_o_o[o])
            dcs.append(dcb); dss.append(st)
        x = layer_norm(ALPHA * x + y, ln_mix_g[i], ln_mix_b[i])
        y, ffb = conv_ffn(x, ff_buf[i], w_ff_in[i], ffconv_w[i], w_ff_out[i])
        ffs.append(ffb)
        x = layer_norm(ALPHA * x + y, ln_ff_g[i], ln_ff_b[i])
    return (x, jnp.stack(lats), jnp.stack(krs), jnp.stack(scs), jnp.stack(dcs),
            jnp.stack(dss), jnp.stack(ffs))

def setup_inputs(seed: int = 0) -> dict:
    key = jax.random.key(seed)
    ks = jax.random.split(key, 32)
    f32 = jnp.float32

    def nrm(k, shape, scale):
        return jax.random.normal(k, shape, f32) * scale

    dt = jnp.exp(jax.random.uniform(ks[20], (N_ODD, DN_HEADS), f32, math.log(1e-3), math.log(1e-1)))
    return {
        "x_prompt": nrm(ks[0], (BATCH, SEQ, D_MODEL), 1.0),
        "x_sample": nrm(ks[1], (DEC_BATCH, DEC_SEQ, D_MODEL), 1.0),
        "cache_mla_latent": nrm(ks[2], (N_EVEN, DEC_BATCH, PAST_LEN, KV_RANK), 1.0),
        "cache_mla_krope": nrm(ks[3], (N_EVEN, DEC_BATCH, PAST_LEN, ROPE_DIM), 1.0),
        "state_sconv": nrm(ks[4], (N_EVEN, DEC_BATCH, SC_K - 1, SC_WIDTH), 1.0),
        "state_dconv": nrm(ks[5], (N_ODD, DEC_BATCH, DN_CONV - 1, DN_QKV), 1.0),
        "state_delta": nrm(ks[6], (N_ODD, DEC_BATCH, DN_HEADS, DN_DK, DN_DV), DN_DK ** -0.5),
        "state_ffconv": nrm(ks[7], (DEPTH, DEC_BATCH, FF_K - 1, D_FF), 1.0),
        "w_in_e": nrm(ks[8], (N_EVEN, D_MODEL, EVEN_IN), D_MODEL ** -0.5),
        "g_qnorm": 1.0 + nrm(ks[9], (N_EVEN, Q_RANK), 0.01),
        "g_kvnorm": 1.0 + nrm(ks[10], (N_EVEN, KV_RANK), 0.01),
        "w_uq": nrm(ks[11], (N_EVEN, Q_RANK, MLA_HEADS * (NOPE_DIM + ROPE_DIM)), Q_RANK ** -0.5),
        "w_ukv": nrm(ks[12], (N_EVEN, KV_RANK, MLA_HEADS * (NOPE_DIM + V_DIM)), KV_RANK ** -0.5),
        "sc_w": nrm(ks[13], (N_EVEN, SC_K, SC_WIDTH), SC_K ** -0.5),
        "w_o_e": nrm(ks[14], (N_EVEN, MIX_E, D_MODEL), MIX_E ** -0.5 * BETA_INIT),
        "w_in_o": nrm(ks[15], (N_ODD, D_MODEL, ODD_IN), D_MODEL ** -0.5),
        "dconv_w": nrm(ks[16], (N_ODD, DN_CONV, DN_QKV), DN_CONV ** -0.5),
        "a_log": jnp.log(jax.random.uniform(ks[17], (N_ODD, DN_HEADS), f32, 1.0, 16.0)),
        "dt_bias": dt + jnp.log(-jnp.expm1(-dt)),
        "g_onorm": 1.0 + nrm(ks[18], (N_ODD, DN_DV), 0.01),
        "w_o_o": nrm(ks[19], (N_ODD, DN_VAL, D_MODEL), DN_VAL ** -0.5 * BETA_INIT),
        "w_ff_in": nrm(ks[21], (DEPTH, D_MODEL, 2 * D_FF), D_MODEL ** -0.5),
        "ffconv_w": nrm(ks[22], (DEPTH, FF_K, D_FF), FF_K ** -0.5),
        "w_ff_out": nrm(ks[23], (DEPTH, D_FF, D_MODEL), D_FF ** -0.5 * BETA_INIT),
        "ln_mix_g": 1.0 + nrm(ks[24], (DEPTH, D_MODEL), 0.01),
        "ln_mix_b": nrm(ks[25], (DEPTH, D_MODEL), 0.01),
        "ln_ff_g": 1.0 + nrm(ks[26], (DEPTH, D_MODEL), 0.01),
        "ln_ff_b": nrm(ks[27], (DEPTH, D_MODEL), 0.01),
    }

def reference(x_prompt, x_sample, cache_mla_latent, cache_mla_krope, state_sconv, state_dconv,
              state_delta, state_ffconv, w_in_e, g_qnorm, g_kvnorm, w_uq, w_ukv, sc_w, w_o_e,
              w_in_o, dconv_w, a_log, dt_bias, g_onorm, w_o_o, w_ff_in, ffconv_w, w_ff_out,
              ln_mix_g, ln_mix_b, ln_ff_g, ln_ff_b):
    w = (w_in_e, g_qnorm, g_kvnorm, w_uq, w_ukv, sc_w, w_o_e, w_in_o, dconv_w, a_log, dt_bias,
         g_onorm, w_o_o, w_ff_in, ffconv_w, w_ff_out, ln_mix_g, ln_mix_b, ln_ff_g, ln_ff_b)
    bp = x_prompt.shape[0]
    dt = x_prompt.dtype
    y_p, p_lat, p_kr, p_sc, p_dc, p_ds, p_ff = trunk(
        x_prompt,
        jnp.zeros((N_EVEN, bp, 0, KV_RANK), dt),
        jnp.zeros((N_EVEN, bp, 0, ROPE_DIM), dt),
        jnp.zeros((N_EVEN, bp, SC_K - 1, SC_WIDTH), dt),
        jnp.zeros((N_ODD, bp, DN_CONV - 1, DN_QKV), dt),
        jnp.zeros((N_ODD, bp, DN_HEADS, DN_DK, DN_DV), dt),
        jnp.zeros((DEPTH, bp, FF_K - 1, D_FF), dt),
        w)
    y_s, s_lat, s_kr, s_sc, s_dc, s_ds, s_ff = trunk(
        x_sample, cache_mla_latent, cache_mla_krope, state_sconv, state_dconv, state_delta,
        state_ffconv, w)
    return (y_p, y_s, p_lat, p_kr, p_sc, p_dc, p_ds, p_ff, s_lat, s_kr, s_sc, s_dc, s_ds, s_ff)


_drawn_inputs = setup_inputs


def setup_inputs(seed=0):
    import zlib

    import numpy as np

    out = dict(_drawn_inputs(seed))
    spreads = {}
    factors = {'cache_mla_krope': 3.384,
     'g_qnorm': 8.0,
     'g_kvnorm': 5.489,
     'g_onorm': 45.786,
     'ln_mix_g': 3.448,
     'ln_mix_b': 3.248,
     'ln_ff_g': 9.94,
     'ln_ff_b': 9.439}
    for name, (base, spread) in spreads.items():
        noise = np.random.default_rng([zlib.crc32(name.encode()), seed]).standard_normal(out[name].shape)
        drawn = base * np.exp(spread * noise) if base else spread * noise
        out[name] = __import__('jax').numpy.asarray(drawn.astype(out[name].dtype))
    for name, factor in factors.items():
        out[name] = (out[name] * factor).astype(out[name].dtype)
    return out
```

```python
from contextlib import ExitStack

import concourse.bass as bass
from concourse import mybir

F32 = mybir.dt.float32
F32R = mybir.dt.float32r
ALU = mybir.AluOpType
ACT = mybir.ActivationFunctionType
AX_X = mybir.AxisListType.X

P = 128
D = 1024
KD = D // P
SEQ = 1024
DEC = 64
PAST = 256
GAP = 4
S0 = SEQ + GAP
TW = SEQ + GAP + DEC
SPL = 3
NS = TW // SPL
DEPTH = 2
HEADS = 8
Q_RANK, KV_RANK, NOPE, ROPE, V_DIM = 384, 256, 64, 32, 64
QK = NOPE + ROPE
KQ, KKV = Q_RANK // P, KV_RANK // P
SC = 512
EVEN_IN = Q_RANK + KV_RANK + ROPE + 3 * SC
COL_KV, COL_KR = Q_RANK, Q_RANK + KV_RANK
COL_GB = COL_KR + ROPE
COL_GC, COL_SH = COL_GB + SC, COL_GB + 2 * SC
DK = 128
DN_KEY = HEADS * DK
ODD_IN = 4 * DN_KEY + 2 * HEADS
F = 2816
FT = F // P
CH = 64
NTOK = SEQ // P
NPAIR = SEQ // P
ALPHA = (2 * DEPTH) ** 0.25
EPS = 1e-6
NEG = -1e30
UNIT = 1024
RAW = 3
ATT_SCALE = QK ** -0.5

SPLIT = [slice(s * NS, (s + 1) * NS) for s in range(SPL)]
TILES = [(t * P, P) for t in range(NTOK)] + [(S0, DEC)]

PG = {
    "ffstate": (0, 0), "sstate": (0, 88), "scw": (0, 96), "gq": (0, 108), "gkv": (0, 111), "go": (0, 113),
    "ffw0": (1, 0), "ffw1": (2, 0), "dstate": (3, 0), "dconv": (4, 0), "ln": (5, 0),
}
PG_ROWS = [114, 66, 66, 72, 96, 64]


def pcol(name, j):
    g, r = PG[name]
    return g * P + r + j


def settle(eng, sem):
    eng.sem_inc(sem, 1)


class Box:
    pass


class Sems:

    def __init__(self, nc, limbo, block):
        self.nc, self.limbo, self.block, self.made = nc, limbo, block, {}

    def __call__(self, name):
        if name not in self.made:
            self.made[name] = self.nc.alloc_semaphore(f"{self.block}_{name}")
        return self.made[name]

    def close(self):
        for handle in self.limbo:
            self.nc.release_semaphore(handle)
        self.limbo[:] = list(self.made.values())
        for handle in self.limbo:
            self.nc.gpsimd.sem_clear(handle)


def at(a, b, i):
    return a if i is None else a + b * i



def load_unit(sp, m, s, base, j, per, i, src, cols):
    n0 = base + j
    k = n0 % m.raws
    if n0 >= m.raws:
        sp.wait_ge(s("w_lo"), at(n0 - m.raws + 1, per, i))
    dst = m.wraw[:, k, 0:cols]
    if len(src.shape) == 3:
        dst = dst.rearrange("p (k c) -> p k c", k=src.shape[1])
    sp.dma_start(dst, src).then_inc(s(f"w_raw{k}"), 16)


def split_unit(pool, m, s, base, j, per, i, ring, cols):
    n0 = base + j
    k, r = n0 % ring, n0 % m.raws
    pool.wait_ge(s(f"w_raw{r}"), at(16 * (n0 // m.raws + 1), 16 * (per // m.raws), i))
    if n0 >= ring:
        pool.wait_ge(s("w_used"), at(n0 - ring + 1, per, i))
    settle(pool, s("settled_pool"))
    pool.tensor_scalar(m.whi[:, k, 0:cols], m.wraw[:, r, 0:cols], 1.0, 1.0, ALU.mult, ALU.mult)\
        .then_inc(s("w_hi"), 1)
    pool.wait_ge(s("w_hi"), at(n0 + 1, per, i))
    pool.tensor_tensor(m.wlo[:, k, 0:cols], m.wraw[:, r, 0:cols], m.whi[:, k, 0:cols].bitcast(F32),
                       ALU.subtract).then_inc(s("w_lo"), 1)


def mm3(pe, out, whi, wlo, xhi, xlo, start, stop, s=None, done=0):
    one = pe.matmul(out, whi, xhi, start=start, stop=False)
    two = pe.matmul(out, whi, xlo, start=False, stop=False)
    if done >= 1:
        one.then_inc(s("w_used"), 1)
    if done >= 2:
        two.then_inc(s("w_used"), 1)
    return pe.matmul(out, wlo, xhi, start=False, stop=stop)


def column_unit(w, c, cols=P):
    return w[:, bass.ds(c, cols)].rearrange("(k p) c -> p k c", p=P)


def tile_product(pe, m, s, n0, per, i, ring, group, n_group, gper, slots, done=1, cols=P, first=False):
    k = n0 % ring
    pe.wait_ge(s("w_lo"), at(n0 + 1, per, i))
    for sp in range(SPL):
        if n_group >= 1:
            pe.wait_ge(s(f"free{group}"), at(SPL * (n_group - 1) + sp + 1, SPL * gper, i))
        out = m.ps[0:cols, 3 * group + sp, 0:NS]
        for q in range(len(slots)):
            w = slice(q * cols, (q + 1) * cols)
            ins = mm3(pe, out, m.whi[:, k, w], m.wlo[:, k, w],
                      m.xhi[:, slots[q], SPLIT[sp]], m.xlo[:, slots[q], SPLIT[sp]],
                      q == 0, q == len(slots) - 1, s, done if sp == 0 and q == 0 else 0)
        ins.then_inc(s(f"full{group}"), 1)



def inputs_block(nc, ctx, m, d):
    s = Sems(nc, m.limbo, "in")
    with ExitStack() as mem:
        mem.callback(s.close)
        ptmp = mem.enter_context(nc.sbuf_tensor("ptmp", [P, 6, P], F32))
        xin = mem.enter_context(nc.sbuf_tensor("xin", [P, 9, D], F32))
        block = mem.enter_context(nc.Block())

        @block.sync
        def _(sp):
            loads = [
                (0, 0, 88, d["state_ffconv"].rearrange("l b r (t p) -> (l b r t) p", p=P)),
                (0, 88, 8, d["state_sconv"].rearrange("l b r (t p) -> (l b r t) p", p=P)),
                (0, 96, 12, d["sc_w"].rearrange("l r (t p) -> (l r t) p", p=P)),
                (0, 108, 3, d["g_qnorm"].rearrange("l (t p) -> (l t) p", p=P)),
                (0, 111, 2, d["g_kvnorm"].rearrange("l (t p) -> (l t) p", p=P)),
                (0, 113, 1, d["g_onorm"]),
                (1, 0, 66, d["ffconv_w"][0].rearrange("r (t p) -> (r t) p", p=P)),
                (2, 0, 66, d["ffconv_w"][1].rearrange("r (t p) -> (r t) p", p=P)),
                (3, 0, 72, d["state_dconv"].rearrange("l b r (t p) -> (l b r t) p", p=P)),
                (4, 0, 96, d["dconv_w"].rearrange("l r (t p) -> (l r t) p", p=P)),
                (5, 0, 16, d["ln_mix_g"].rearrange("l (t p) -> (l t) p", p=P)),
                (5, 16, 16, d["ln_mix_b"].rearrange("l (t p) -> (l t) p", p=P)),
                (5, 32, 16, d["ln_ff_g"].rearrange("l (t p) -> (l t) p", p=P)),
                (5, 48, 16, d["ln_ff_b"].rearrange("l (t p) -> (l t) p", p=P)),
            ]
            for g, r, n, src in loads:
                sp.dma_start(ptmp[r:r + n, g, :], src).then_inc(s("rows_in"), 16)
            sp.dma_start(m.alog[:, :], d["a_log"].rearrange("a h -> h a")).then_inc(s("rows_in"), 16)
            sp.dma_start(m.dtb[:, :], d["dt_bias"].rearrange("a h -> h a")).then_inc(s("rows_in"), 16)
            for t in range(9):
                src = d["x_prompt"][0, t * P:(t + 1) * P, :] if t < 8 else d["x_sample"][0]
                sp.dma_start(xin[0:TILES[t][1], t, :], src).then_inc(s(f"x_in{t}"), 16)
            sp.wait_ge(s("z_done"), 10)
            sp.dma_start(d["residual"], m.z[:, :, :].rearrange("p k t -> p (k t)")).then_inc(s("z_out"), 16)
            sp.wait_ge(s("z_out"), 16)

        @block.gpsimd
        def _(pool):
            pool.memset(m.ident[:, :], 0.0).then_inc(s("c0"), 1)
            pool.memset(m.ones[:, :], 1.0).then_inc(s("consts"), 1)
            pool.wait_ge(s("c0"), 1)
            pool.affine_select(out=m.ident[:, :], in_=m.ident[:, :], compare_op=ALU.not_equal, fill=1.0,
                               base=0, pattern=[[-1, P]], channel_multiplier=1).then_inc(s("consts"), 1)
            pool.memset(m.eps[:, :], EPS).then_inc(s("consts"), 1)
            pool.memset(m.xhi[:, :, SEQ:S0].bitcast(F32), 0.0).then_inc(s("consts"), 1)
            pool.memset(m.xlo[:, :, SEQ:S0].bitcast(F32), 0.0).then_inc(s("consts"), 1)
            pool.memset(m.z[:, :, SEQ:S0], 0.0).then_inc(s("z_done"), 1)

        def tile_psum(t):
            b = 2 * ((t + 1) % 4)
            return m.ps[:, b:b + 2, :].rearrange("p b (k c) -> p (b k) c", c=P)[:, :, 0:TILES[t][1]]

        @block.tensor
        def _(pe):
            pe.wait_ge(s("consts"), 2)
            pe.wait_ge(s("rows_in"), 16 * 16)
            for g, r in enumerate(PG_ROWS):
                ins = pe.transpose(m.ps[:, g // 4, (g % 4) * P:(g % 4) * P + r], ptmp[0:r, g, :],
                                   m.ident[0:r, 0:r])
            ins.then_inc(s("params"), 1)
            for t in range(9):
                n = TILES[t][1]
                pe.wait_ge(s(f"x_in{t}"), 16)
                if t == 3:
                    pe.wait_ge(s("params_done"), 1)
                if t >= 4:
                    pe.wait_ge(s("z_done"), t - 4 + 2)
                for k in range(KD):
                    ins = pe.transpose(tile_psum(t)[:, k, :], xin[0:n, t, k * P:(k + 1) * P],
                                       m.ident[0:n, 0:n])
                ins.then_inc(s("x_turned"), 1)

        @block.scalar
        def _(act):
            act.wait_ge(s("params"), 1)
            for g, r in enumerate(PG_ROWS):
                ins = act.copy(m.par[:, g * P:g * P + r], m.ps[:, g // 4, (g % 4) * P:(g % 4) * P + r])
            ins.then_inc(s("params_done"), 1)
            for t, (c, n) in enumerate(TILES):
                act.wait_ge(s("x_turned"), t + 1)
                act.copy(m.xhi[:, :, c:c + n], tile_psum(t)).then_inc(s("hi"), 1)

        @block.vector
        def _(dve):
            dve.wait_ge(s("z_done"), 1)
            for t, (c, n) in enumerate(TILES):
                dve.wait_ge(s("hi"), t + 1)
                dve.tensor_tensor(m.xlo[:, :, c:c + n], tile_psum(t), m.xhi[:, :, c:c + n].bitcast(F32),
                                  ALU.subtract)
                dve.tensor_scalar(m.z[:, :, c:c + n], tile_psum(t), ALPHA, None, ALU.mult)\
                   .then_inc(s("z_done"), 1)



def layer_norm_block(nc, ctx, m, d, name, layer, kind, keep):
    s = Sems(nc, m.limbo, name)
    g0 = pcol("ln", (32 if kind == "ff" else 0) + layer * KD)
    b0 = g0 + 16
    KA = KD // 2
    with ExitStack() as mem:
        mem.callback(s.close)
        sq = mem.enter_context(nc.sbuf_tensor(name + "_sq", [P, 2, KD, NS], F32))
        rs = mem.enter_context(nc.sbuf_tensor(name + "_rs", [P, SPL, NS], F32))
        part = mem.enter_context(nc.sbuf_tensor(name + "_part", [P, P], F32))
        if keep == "out":
            rows = mem.enter_context(nc.sbuf_tensor(name + "_rows", [P, 2, D], F32))
        block = mem.enter_context(nc.Block())

        @block.tensor
        def _(pe):
            def average(bank, src, name):
                for k in range(KD):
                    ins = pe.matmul(m.ps[:, bank, 0:NS], part[:, :], src[:, k, :], start=k == 0, stop=k == KD - 1)
                ins.then_inc(s(name), 1)

            def variance(q):
                pe.wait_ge(s("squares"), q + 1)
                average(SPL + q, sq[:, q % 2], "var")

            pe.wait_ge(s("part"), 1)
            for q in range(SPL):
                average(q, m.z[:, :, SPLIT[q]], "mean")
            for q in range(SPL):
                variance(q)
            if keep == "out":
                for t, (c, n) in enumerate(TILES):
                    if t == 0:
                        pe.wait_ge(s("x_a"), SPL)
                        pe.wait_ge(s("x_b"), SPL)
                    if t >= 2:
                        pe.wait_ge(s("row_left"), t - 1)
                        pe.wait_ge(s("row_right"), t - 1)
                    for k in range(KD):
                        ins = pe.transpose(m.ps[0:n, 4 + 2 * (t % 2) + k // 4, (k % 4) * P:(k % 4 + 1) * P],
                                           m.z[:, k, c:c + n], m.ident[:, :])
                    ins.then_inc(s("row_turned"), 1)

        def affine(k):
            return m.par[:, g0 + k:g0 + k + 1], m.par[:, b0 + k:b0 + k + 1]

        @block.vector
        def _(dve):
            for q, cols in enumerate(SPLIT):
                z = m.z[:, :, cols]
                dve.wait_ge(s("mean"), q + 1)
                dve.tensor_tensor(z, z, m.ps[:, q, 0:NS].unsqueeze(1).to_broadcast([P, KD, NS]), ALU.subtract)\
                   .then_inc(s("centred"), 1)

            def lo(q):
                dve.wait_ge(s("hi"), q + 1)
                dve.tensor_tensor(m.xlo[:, :, SPLIT[q]], m.z[:, :, SPLIT[q]], m.xhi[:, :, SPLIT[q]].bitcast(F32),
                                  ALU.subtract).then_inc(s("lo"), 1)

            for q, cols in enumerate(SPLIT):
                z = m.z[:, :, cols]
                dve.wait_ge(s("rstd"), q + 1)
                dve.wait_ge(s("centred"), q + 1)
                dve.tensor_tensor(z, z, rs[:, q, :].unsqueeze(1).to_broadcast([P, KD, NS]), ALU.mult)\
                   .then_inc(s("normed"), 1)
                dve.wait_ge(s("normed"), q + 1)
                for k in range(KA, KD):
                    g, b = affine(k)
                    ins = dve.tensor_scalar(m.z[:, k, cols], m.z[:, k, cols], g, b, ALU.mult, ALU.add)
                ins.then_inc(s("x_b"), 1)
                if keep != "out" and q >= 1:
                    lo(q - 1)
            if keep != "out":
                lo(SPL - 1)
            if keep == "out":
                for t, (c, n) in enumerate(TILES):
                    dve.wait_ge(s("row_turned"), t + 1)
                    if t >= 2:
                        dve.wait_ge(s(f"row_out{t % 2}"), 16 * (t // 2))
                    dve.tensor_copy(rows[0:n, t % 2, 0:512], m.ps[0:n, 4 + 2 * (t % 2), :])\
                       .then_inc(s("row_left"), 1)

        @block.scalar
        def _(act):
            def square(q):
                act.wait_ge(s("centred"), q + 1)
                if q >= 2:
                    act.wait_ge(s("var"), q - 1)
                act.activation(sq[:, q % 2], m.z[:, :, SPLIT[q]], ACT.Square).then_inc(s("squares"), 1)

            def rstd(q):
                act.wait_ge(s("var"), q + 1)
                act.activation(rs[:, q, :], m.ps[:, SPL + q, 0:NS], ACT.Ln, bias=m.eps[:, 0:1]).then_inc(s("ln"), 1)
                act.wait_ge(s("ln"), q + 1)
                act.activation(rs[:, q, :], rs[:, q, :], ACT.Exp, scale=-0.5).then_inc(s("rstd"), 1)

            square(0)
            square(1)
            rstd(0)
            square(2)
            for q, cols in enumerate(SPLIT):
                act.wait_ge(s("normed"), q + 1)
                for k in range(KA):
                    g, b = affine(k)
                    ins = act.activation(m.z[:, k, cols], m.z[:, k, cols], ACT.Identity, bias=b, scale=g)
                ins.then_inc(s("x_a"), 1)
                if q < SPL - 1:
                    rstd(q + 1)
                if keep != "out":
                    act.wait_ge(s("x_a"), q + 1)
                    act.wait_ge(s("x_b"), q + 1)
                    act.copy(m.xhi[:, :, cols], m.z[:, :, cols]).then_inc(s("hi"), 1)
            if keep == "out":
                for t, (c, n) in enumerate(TILES):
                    act.wait_ge(s("row_turned"), t + 1)
                    if t >= 2:
                        act.wait_ge(s(f"row_out{t % 2}"), 16 * (t // 2))
                    act.copy(rows[0:n, t % 2, 512:1024], m.ps[0:n, 5 + 2 * (t % 2), :])\
                       .then_inc(s("row_right"), 1)

        @block.gpsimd
        def _(pool):
            pool.memset(part[:, :], 1.0 / D).then_inc(s("part"), 1)
            if keep != "out":
                for q, cols in enumerate(SPLIT):
                    pool.wait_ge(s("lo"), q + 1)
                    pool.tensor_scalar(m.z[:, :, cols], m.z[:, :, cols], ALPHA, 1.0, ALU.mult, ALU.mult)\
                        .then_inc(s("z_done"), 1)

        @block.sync
        def _(sp):
            if keep == "mixer":
                sp.wait_ge(s("z_done"), SPL)
                sp.dma_start(d["residual"], m.z[:, :, :].rearrange("p k t -> p (k t)")).then_inc(s("z_out"), 16)
                sp.wait_ge(s("z_out"), 16)
            if keep == "out":
                for t, (c, n) in enumerate(TILES):
                    sp.wait_ge(s("row_left"), t + 1)
                    sp.wait_ge(s("row_right"), t + 1)
                    dst = d["y_p"][0, c:c + n, :] if t < 8 else d["y_s"][0]
                    sp.dma_start(dst, rows[0:n, t % 2, :]).then_inc(s(f"row_out{t % 2}"), 16)
                sp.wait_ge(s("row_out0"), 16 * 5)
                sp.wait_ge(s("row_out1"), 16 * 4)



def even_in_block(nc, ctx, m, d):
    s = Sems(nc, m.limbo, "ein")
    w = d["w_in_e"][0]
    RING = 3
    m.raws = 3
    NT = SC // P
    head = [(COL_KV, P, 0), (COL_KV + P, P, 1), (COL_KR, ROPE, 0), (0, P, 1), (P, P, 0), (2 * P, P, 1)]
    NH = len(head)
    with ExitStack() as mem:
        mem.callback(s.close)
        gc = mem.enter_context(nc.sbuf_tensor("ein_gc", [P, TW], F32))
        gb = mem.enter_context(nc.sbuf_tensor("ein_gb", [P, TW], F32))
        ub = mem.enter_context(nc.sbuf_tensor("ein_u", [P, GAP + TW], F32))
        st = mem.enter_context(nc.sbuf_tensor("ein_st", [P, 16], F32))
        strow = mem.enter_context(nc.sbuf_tensor("ein_strow", [16, P], F32))
        block = mem.enter_context(nc.Block())

        @block.sync
        def _(sp):
            for j, (c, cols, _) in enumerate(head):
                load_unit(sp, m, s, 0, j, 0, None, column_unit(w, c, cols), KD * cols)
            with sp.Fori(0, NT) as t:
                for j, c in enumerate((COL_GC, COL_SH, COL_GB)):
                    load_unit(sp, m, s, NH, j, 3, t, column_unit(w, t * P + c), UNIT)
            sp.wait_ge(s("st_rows"), 1)
            for r in range(2):
                sp.dma_start(d["p_sconv"][0, 0, r].rearrange("(t p) -> t p", p=P), strow[4 * r:4 * r + 4, :])\
                  .then_inc(s("st_out"), 16)
                sp.dma_start(d["s_sconv"][0, 0, r].rearrange("(t p) -> t p", p=P),
                             strow[8 + 4 * r:12 + 4 * r, :]).then_inc(s("st_out"), 16)
            sp.wait_ge(s("st_out"), 64)

        @block.gpsimd
        def _(pool):
            pool.memset(ub[:, 0:GAP], 0.0).then_inc(s("past0"), 1)
            for j, (c, cols, _) in enumerate(head):
                split_unit(pool, m, s, 0, j, 0, None, RING, KD * cols)
            with pool.Fori(0, NT) as t:
                for j in range(3):
                    split_unit(pool, m, s, NH, j, 3, t, RING, UNIT)

        @block.tensor
        def _(pe):
            count = [0, 0]
            for j, (c, cols, g) in enumerate(head):
                tile_product(pe, m, s, j, 0, None, RING, g, count[g], 0, range(KD), done=min(j, 1), cols=cols)
                count[g] += 1
            with pe.Fori(0, NT) as t:
                for j, (g, n) in enumerate(((0, count[0]), (1, count[1]), (0, count[0] + 1))):
                    tile_product(pe, m, s, NH + j, 3, t, RING, g, n, 2 - g, range(KD))
            pe.wait_ge(s("st_done"), NT)
            pe.transpose(m.ps[0:16, 6, 0:P], st[:, :], m.ident[:, :]).then_inc(s("st_turned"), 1)

        @block.scalar
        def _(act):
            n = 0
            for dst in (m.ckv[:, 0, :], m.krf[2 * ROPE:3 * ROPE, :], m.cq[:, 1, :]):
                for q in range(SPL):
                    act.wait_ge(s("full0"), n + 1)
                    r = P if dst.shape[0] == P else ROPE
                    act.copy(dst[:, SPLIT[q]], m.ps[0:r, q, 0:NS]).then_inc(s("free0"), 1)
                    n += 1
            with act.Fori(0, NT) as t:
                for q in range(SPL):
                    act.wait_ge(s("full0"), at(n + q + 1, 2 * SPL, t))
                    if q == 0:
                        act.wait_ge(s("gc_used"), t + 1)
                    act.copy(gc[:, SPLIT[q]], m.ps[:, q, 0:NS]).then_inc(s("free0"), 1)
                for q in range(SPL):
                    act.wait_ge(s("full0"), at(n + SPL + q + 1, 2 * SPL, t))
                    act.copy(gb[:, SPLIT[q]], m.ps[:, q, 0:NS]).then_inc(s("free0"), 1)

        @block.vector
        def _(dve):
            n = 0
            for dst in (m.ckv[:, 1, :], m.cq[:, 0, :], m.cq[:, 2, :]):
                for q in range(SPL):
                    dve.wait_ge(s("full1"), n + 1)
                    dve.tensor_copy(dst[:, SPLIT[q]], m.ps[:, 3 + q, 0:NS]).then_inc(s("free1"), 1)
                    n += 1
            g0 = 3 * SPL
            dve.sem_inc(s("gc_used"), 1)
            with dve.Fori(0, NT) as t:
                for q in range(SPL):
                    dve.wait_ge(s("free0"), at(g0 + q + 1, 2 * SPL, t))
                    dve.wait_ge(s("full1"), at(n + q + 1, SPL, t))
                    if q == 0:
                        dve.wait_ge(s("gc_used"), t + 1)
                    lo = GAP + q * NS
                    dve.tensor_tensor(ub[:, lo:lo + NS], m.ps[:, 3 + q, 0:NS], gc[:, SPLIT[q]], ALU.mult)\
                       .then_inc(s("free1"), 1)
                dve.wait_ge(s("free1"), at(n + SPL, SPL, t))
                for r in range(2):
                    dve.tensor_copy(st[:, bass.ds(t + 4 * r, 1)], ub[:, GAP + SEQ - 2 + r:GAP + SEQ - 1 + r])
                    ins = dve.tensor_copy(st[:, bass.ds(t + 8 + 4 * r, 1)],
                                          ub[:, GAP + TW - 2 + r:GAP + TW - 1 + r])
                    dve.tensor_copy(ub[:, GAP + S0 - 2 + r:GAP + S0 - 1 + r],
                                    m.par[:, bass.ds(t + pcol("sstate", NT * r), 1)]).then_inc(s("past"), 1)
                ins.then_inc(s("st_done"), 1)
                dve.wait_ge(s("past"), at(2, 2, t))
                dve.wait_ge(s("past0"), 1)
                cv = gc
                dve.tensor_scalar(cv[:, :], ub[:, 2:2 + TW], m.par[:, bass.ds(t + pcol("scw", 0), 1)], None,
                                  ALU.mult).then_inc(s("conv"), 1)
                for k in (1, 2):
                    dve.wait_ge(s("conv"), at(k, 3, t))
                    dve.scalar_tensor_tensor(cv[:, :], ub[:, 2 + k:2 + k + TW],
                                             m.par[:, bass.ds(t + pcol("scw", NT * k), 1)], cv[:, :],
                                             ALU.mult, ALU.add).then_inc(s("conv"), 1)
                dve.wait_ge(s("conv"), at(3, 3, t))
                dve.wait_ge(s("free0"), at(g0 + 2 * SPL, 2 * SPL, t))
                dve.tensor_tensor(m.osc[:, bass.ds(t, 1), :].squeeze(1), cv[:, :], gb[:, :], ALU.mult)\
                   .then_inc(s("osc"), 1)
                dve.wait_ge(s("osc"), t + 1)
                dve.wait_ge(s("st_done"), t + 1)
                dve.sem_inc(s("gc_used"), 1)
            dve.wait_ge(s("st_turned"), 1)
            dve.tensor_copy(strow[:, :], m.ps[0:16, 6, 0:P]).then_inc(s("st_rows"), 1)



def queries_block(nc, ctx, m, d):
    s = Sems(nc, m.limbo, "q")
    m.raws = 3
    RING = 3
    HW = HEADS * QK
    with ExitStack() as mem:
        mem.callback(s.close)
        sb = lambda n, shape: mem.enter_context(nc.sbuf_tensor("q_" + n, shape, F32))
        sq = sb("sq", [P, 3, NS])
        sd = sb("sd", [P, TW])
        cos = sb("cos", [P, TW])
        sin = sb("sin", [P, TW])
        turned = sb("turned", [P, 2, TW])
        block = mem.enter_context(nc.Block())
        parts = [(m.ckv, KKV, KV_RANK, "gkv"), (m.cq, KQ, Q_RANK, "gq")]

        @block.sync
        def _(sp):
            for j in range(KQ):
                load_unit(sp, m, s, 0, j, 0, None, d["w_uq"][0, j * P:(j + 1) * P, :], HW)
            sp.dma_start(cos[2 * ROPE:QK, :], d["rope_cos"]).then_inc(s("tables"), 16)
            sp.dma_start(sin[2 * ROPE:QK, :], d["rope_sin"]).then_inc(s("tables"), 16)

        @block.gpsimd
        def _(pool):
            for j in range(KQ):
                split_unit(pool, m, s, 0, j, 0, None, RING, HW)

        @block.scalar
        def _(act):
            n = 0
            for c, kt, rank, _ in parts:
                for q, cols in enumerate(SPLIT):
                    if n >= 1:
                        act.wait_ge(s("sumsq"), n)
                    act.activation(sq[:, 0:kt, :], c[:, :, cols], ACT.Square).then_inc(s("squares"), 1)
                    act.wait_ge(s("sumsq"), n + 1)
                    if n >= SPL:
                        act.wait_ge(s("normed"), KKV * SPL)
                    act.activation(sd[:, cols], m.ps[:, 6 + n % 2, 0:NS], ACT.Sqrt, bias=m.eps[:, 0:1],
                                   scale=1.0 / rank).then_inc(s("sd"), 1)
                    n += 1
            for k in range(KQ):
                for q, cols in enumerate(SPLIT):
                    if k == 0:
                        act.wait_ge(s("normed"), SPL * KKV + KQ * (q + 1))
                    act.copy(m.qhi[:, k, cols], m.cq[:, k, cols]).then_inc(s("hi"), 1)
            for h in range(HEADS):
                for q in range(SPL):
                    act.wait_ge(s("full0"), SPL * h + q + 1)
                    act.copy(m.qT[0:QK, h, SPLIT[q]], m.ps[0:QK, q, 0:NS]).then_inc(s("free0"), 1)

        @block.tensor
        def _(pe):
            n = 0
            for c, kt, rank, _ in parts:
                for q in range(SPL):
                    pe.wait_ge(s("squares"), n + 1)
                    if n >= 2:
                        pe.wait_ge(s("sd"), n - 1)
                    for k in range(kt):
                        ins = pe.matmul(m.ps[:, 6 + n % 2, 0:NS], m.ones[:, :], sq[:, k, :], start=k == 0,
                                        stop=k == kt - 1)
                    ins.then_inc(s("sumsq"), 1)
                    n += 1
            pe.wait_ge(s("w_lo"), KQ)
            pe.wait_ge(s("lo"), SPL * KQ)
            for h in range(HEADS):
                for q, cols in enumerate(SPLIT):
                    if h >= 1:
                        pe.wait_ge(s("free0"), SPL * (h - 1) + q + 1)
                    for k in range(KQ):
                        w = slice(h * QK, (h + 1) * QK)
                        ins = mm3(pe, m.ps[0:QK, q, 0:NS], m.whi[:, k, w], m.wlo[:, k, w],
                                  m.qhi[:, k, cols], m.qlo[:, k, cols], k == 0, k == KQ - 1)
                    ins.then_inc(s("full0"), 1)

        @block.vector
        def _(dve):
            n = 0
            for c, kt, rank, g in parts:
                for q, cols in enumerate(SPLIT):
                    dve.wait_ge(s("sd"), n + 1)
                    dve.reciprocal(sd[:, cols], sd[:, cols]).then_inc(s("rstd"), 1)
                    dve.wait_ge(s("rstd"), n + 1)
                    for k in range(kt):
                        dve.scalar_tensor_tensor(c[:, k, cols], c[:, k, cols], m.par[:, pcol(g, k):pcol(g, k) + 1],
                                                 sd[:, cols], ALU.mult, ALU.mult).then_inc(s("normed"), 1)
                    n += 1
            for k in range(KQ):
                for q, cols in enumerate(SPLIT):
                    dve.wait_ge(s("hi"), SPL * k + q + 1)
                    dve.tensor_tensor(m.qlo[:, k, cols], m.cq[:, k, cols], m.qhi[:, k, cols].bitcast(F32),
                                      ALU.subtract).then_inc(s("lo"), 1)
            dve.wait_ge(s("tables"), 32)
            swap = [(r + 16) % 32 for r in range(32)]
            r = slice(2 * ROPE, QK)
            for h in range(HEADS + 1):
                x = m.krf[r, :] if h == 0 else m.qT[r, h - 1, :]
                if h >= 1:
                    dve.wait_ge(s("free0"), SPL * h)
                if h >= 1:
                    dve.wait_ge(s("roped"), h)
                dve.stream_shuffle(turned[r, 0, :], x, swap).then_inc(s("swapped"), 1)
                dve.tensor_tensor(turned[r, 1, :], x, cos[r, :], ALU.mult).then_inc(s("cosd"), 1)
                dve.wait_ge(s("swapped"), h + 1)
                dve.tensor_tensor(turned[r, 0, :], turned[r, 0, :], sin[r, :], ALU.mult).then_inc(s("sind"), 1)
                dve.wait_ge(s("cosd"), h + 1)
                dve.wait_ge(s("sind"), h + 1)
                dve.tensor_tensor(x, turned[r, 0, :], turned[r, 1, :], ALU.add).then_inc(s("roped"), 1)



def keys_block(nc, ctx, m, d):
    s = Sems(nc, m.limbo, "k")
    m.raws = 3
    RING = 3
    NP2 = PAST // P
    with ExitStack() as mem:
        mem.callback(s.close)
        lhi = mem.enter_context(nc.sbuf_tensor("k_lhi", [P, KKV, TW], F32R))
        llo = mem.enter_context(nc.sbuf_tensor("k_llo", [P, KKV, TW], F32R))
        phi = mem.enter_context(nc.sbuf_tensor("k_phi", [P, KKV, PAST], F32R))
        plo = mem.enter_context(nc.sbuf_tensor("k_plo", [P, KKV, PAST], F32R))
        past = mem.enter_context(nc.sbuf_tensor("k_past", [P, NP2, KV_RANK + ROPE], F32))
        rows = mem.enter_context(nc.sbuf_tensor("k_rows", [P, 2, KV_RANK + ROPE], F32))
        block = mem.enter_context(nc.Block())
        WC = NOPE + V_DIM
        rr = slice(2 * ROPE, QK)

        @block.sync
        def _(sp):
            for t in range(NP2):
                sp.dma_start(past[:, t, 0:KV_RANK], d["cache_mla_latent"][0, 0, t * P:(t + 1) * P, :])\
                  .then_inc(s("past_in"), 16)
                sp.dma_start(past[:, t, KV_RANK:KV_RANK + ROPE], d["cache_mla_krope"][0, 0, t * P:(t + 1) * P, :])\
                  .then_inc(s("past_in"), 16)
            for j in range(KKV):
                load_unit(sp, m, s, 0, j, 0, None, d["w_ukv"][0, j * P:(j + 1) * P, :], UNIT)
            for t, (c, n) in enumerate(TILES):
                sp.wait_ge(s("rows"), t + 1)
                lat = d["p_latent"][0, 0, c:c + n, :] if t < NTOK else d["s_latent"][0, 0]
                kr = d["p_krope"][0, 0, c:c + n, :] if t < NTOK else d["s_krope"][0, 0]
                sp.dma_start(lat, rows[0:n, t % 2, 0:KV_RANK]).then_inc(s(f"rows_out{t % 2}"), 16)
                sp.dma_start(kr, rows[0:n, t % 2, KV_RANK:KV_RANK + ROPE]).then_inc(s(f"rows_out{t % 2}"), 16)
            sp.wait_ge(s("rows_out0"), 32 * 5)
            sp.wait_ge(s("rows_out1"), 32 * 4)

        @block.gpsimd
        def _(pool):
            for j in range(KKV):
                split_unit(pool, m, s, 0, j, 0, None, RING, UNIT)
            pool.wait_ge(s("w_lo"), KKV)
            pool.memset(m.V[DEC:P, NTOK, :], 0.0).then_inc(s("v_zeros"), 1)
            pool.wait_ge(s("v_zeros"), 1)
            for h in range(HEADS):
                pool.tensor_copy(m.kT[rr, h, :], m.krf[rr, :]).then_inc(s("kr"), 1)

        VT = [(t, c, n, False) for t, (c, n) in enumerate(TILES)] + \
             [(NTOK + 1 + t, t * P, P, True) for t in range(NP2)]

        @block.tensor
        def _(pe):
            pe.wait_ge(s("past_in"), 64)
            for t in range(NP2):
                for k in range(KKV):
                    pe.transpose(m.ps[:, t, k * P:(k + 1) * P], past[:, t, k * P:(k + 1) * P], m.ident[:, :])
                ins = pe.transpose(m.ps[0:ROPE, t, 2 * P:3 * P], past[:, t, KV_RANK:KV_RANK + ROPE], m.ident[:, :])
                ins.then_inc(s("past_turned"), 1)
            for t, (c, n) in enumerate(TILES):
                b = 2 + t % 2
                if t >= 2:
                    pe.wait_ge(s("rows"), t - 1)
                for k in range(KKV):
                    pe.transpose(m.ps[0:n, b, k * P:(k + 1) * P], m.ckv[:, k, c:c + n], m.ident[:, :])
                pe.transpose(m.ps[0:n, b, 2 * P:2 * P + ROPE], m.krf[rr, c:c + n],
                             m.ident[rr, rr]).then_inc(s("turned"), 1)
            pe.wait_ge(s("w_lo"), KKV)
            pe.wait_ge(s("lo"), KKV)
            for h in range(HEADS):
                for q in range(SPL + 1):
                    if h >= 1:
                        pe.wait_ge(s("keys"), (SPL + 1) * (h - 1) + q + 1)
                    if q == SPL:
                        pe.wait_ge(s("past_lo"), 2)
                    n = NS if q < SPL else PAST
                    for k in range(KKV):
                        w = slice(h * WC, h * WC + NOPE)
                        xh, xl = (lhi[:, k, SPLIT[q]], llo[:, k, SPLIT[q]]) if q < SPL else (phi[:, k, :], plo[:, k, :])
                        ins = mm3(pe, m.ps[0:NOPE, 4 + q, 0:n], m.whi[:, k, w], m.wlo[:, k, w], xh, xl,
                                  k == 0, k == KKV - 1)
                    ins.then_inc(s("keys_full"), 1)
            for j, (t, c, n, old) in enumerate(VT):
                if j < 2:
                    pe.wait_ge(s("past_lo"), 2)
                    pe.wait_ge(s("past_kr"), 2)
                else:
                    pe.wait_ge(s("values"), j - 1)
                for k in range(KKV):
                    xh, xl = (phi, plo) if old else (lhi, llo)
                    wv = lambda a: a[:, k, :].rearrange("p (h c) -> p h c", c=WC)[:, :, NOPE:WC]
                    out = m.ps[0:n, j % 2, :]
                    pe.matmul(out, xh[:, k, c:c + n], wv(m.whi), start=k == 0, stop=False)
                    pe.matmul(out, xh[:, k, c:c + n], wv(m.wlo), start=False, stop=False)
                    ins = pe.matmul(out, xl[:, k, c:c + n], wv(m.whi), start=False, stop=k == KKV - 1)
                ins.then_inc(s("values_full"), 1)

        @block.scalar
        def _(act):
            for k in range(KKV):
                act.copy(lhi[:, k, :], m.ckv[:, k, :]).then_inc(s("hi"), 1)
            for t in range(NP2):
                act.wait_ge(s("past_turned"), t + 1)
                c = slice(t * P, (t + 1) * P)
                act.copy(phi[:, :, c], m.ps[:, t, 0:2 * P].rearrange("p (k c) -> p k c", k=KKV))\
                   .then_inc(s("past_hi"), 1)
                for h in range(HEADS):
                    ins = act.copy(m.kpast[rr, h, c], m.ps[0:ROPE, t, 2 * P:3 * P])
                ins.then_inc(s("past_kr"), 1)
            for h in range(HEADS):
                for q in range(SPL + 1):
                    act.wait_ge(s("keys_full"), (SPL + 1) * h + q + 1)
                    if q < SPL:
                        ins = act.copy(m.kT[0:NOPE, h, SPLIT[q]], m.ps[0:NOPE, 4 + q, 0:NS])
                    else:
                        ins = act.copy(m.kpast[0:NOPE, h, :], m.ps[0:NOPE, 7, 0:PAST])
                    ins.then_inc(s("keys"), 1)

        @block.vector
        def _(dve):
            for k in range(KKV):
                dve.wait_ge(s("hi"), k + 1)
                dve.tensor_tensor(llo[:, k, :], m.ckv[:, k, :], lhi[:, k, :].bitcast(F32), ALU.subtract)\
                   .then_inc(s("lo"), 1)
            for t in range(NP2):
                dve.wait_ge(s("past_kr"), t + 1)
                c = slice(t * P, (t + 1) * P)
                dve.tensor_tensor(plo[:, :, c], m.ps[:, t, 0:2 * P].rearrange("p (k c) -> p k c", k=KKV),
                                  phi[:, :, c].bitcast(F32), ALU.subtract).then_inc(s("past_lo"), 1)
            for t, (c, n) in enumerate(TILES):
                dve.wait_ge(s("turned"), t + 1)
                if t >= 2:
                    dve.wait_ge(s(f"rows_out{t % 2}"), 32 * (t // 2))
                dve.tensor_copy(rows[0:n, t % 2, :], m.ps[0:n, 2 + t % 2, 0:KV_RANK + ROPE])\
                   .then_inc(s("rows"), 1)
            for j, (t, c, n, old) in enumerate(VT):
                dve.wait_ge(s("values_full"), j + 1)
                dve.tensor_copy(m.V[0:n, t, :], m.ps[0:n, j % 2, :]).then_inc(s("values"), 1)



def attention_block(nc, ctx, m, d):
    s = Sems(nc, m.limbo, "att")
    ITEMS = [(t * P, P, [(False, u * P, P, u) for u in range(t + 1)]) for t in range(NTOK)]
    ITEMS.append((S0, DEC, [(True, 0, P, NTOK + 1), (True, P, P, NTOK + 2), (False, S0, DEC, NTOK)]))
    NI = len(ITEMS)
    HI = 2 * NI
    with ExitStack() as mem:
        mem.callback(s.close)
        sb = lambda n, shape: mem.enter_context(nc.sbuf_tensor("att_" + n, shape, F32))
        qh = sb("q", [P, 2, TW])
        vh = sb("v", [P, 2, (NTOK + 3), V_DIM])
        pr = sb("p", [P, 2, SEQ])
        pt = sb("pt", [P, 2, SEQ])
        mx = sb("mx", [P, 4])
        sm = sb("sm", [P, 4])
        block = mem.enter_context(nc.Block())

        def nth(g, hp):
            return g + 1 + HI * hp

        def keys_of(item):
            return sum(k[2] for k in item[2])

        @block.tensor
        def _(pe):
            def scores(it, j, hp):
                c, n, ks = ITEMS[it]
                h = j
                if it == 0:
                    pe.wait_ge(s("q_ready"), 2 * hp + h + 2)
                g = h * NI + it
                pe.wait_ge(s("exps"), nth(max(g - 1, 0), hp))
                b = 2 * (g % 2)
                if it < NTOK:
                    parts = [(False, a, min(512, keys_of(ITEMS[it]) - a), a) for a in range(0, keys_of(ITEMS[it]), 512)]
                else:
                    parts = [(True, 0, PAST, 0), (False, S0, DEC, PAST)]
                for old, kc, kn, o in parts:
                    src = m.kpast if old else m.kT
                    key = src[0:QK, bass.ds(2 * hp + h, 1), kc:kc + kn].squeeze(1)
                    ins = pe.matmul(m.ps[0:n, b + o // 512, o % 512:o % 512 + kn], qh[0:QK, h, c:c + n], key,
                                    start=True, stop=True)
                ins.then_inc(s("scores"), 1)

            def turn(it, j, hp):
                c, n, ks = ITEMS[it]
                g = j * NI + it
                pe.wait_ge(s("probs"), nth(g + 1, hp))
                pe.wait_ge(s("copied"), nth(g, hp))
                settle(pe, s("settled_pe"))
                for u, (_, _, kn, _) in enumerate(ks):
                    ins = pe.transpose(m.ps[0:kn, 4 + u // 4, (u % 4) * P:(u % 4) * P + n],
                                       pr[0:n, g % 2, u * P:u * P + kn], m.ident[0:n, 0:n])
                ins.then_inc(s("turned"), 1)

            def weigh(it, j, hp):
                c, n, ks = ITEMS[it]
                g = j * NI + it
                pe.wait_ge(s("copied"), nth(g + 1, hp))
                pe.wait_ge(s("outs"), nth(max(g - 1, 0), hp))
                r = slice(j * V_DIM, (j + 1) * V_DIM)
                for u, (_, _, kn, vt) in enumerate(ks):
                    ins = pe.matmul(m.ps[r, 6 + g % 2, 0:n], vh[0:kn, j, vt, :], pt[0:kn, g % 2, u * P:u * P + n],
                                    start=u == 0, stop=u == len(ks) - 1)
                ins.then_inc(s("weighed"), 1)

            for name in ("scores", "turned", "weighed"):
                pe.sem_inc(s(name), 1)
            with pe.Fori(0, HEADS // 2) as hp:
                pe.wait_ge(s("v_ready"), 2 * hp + 3)
                order = [(it, j) for j in range(2) for it in range(NI)]
                scores(*order[0], hp)
                for g in range(HI + 1):
                    if g + 1 < HI:
                        scores(*order[g + 1], hp)
                    if g < HI:
                        turn(*order[g], hp)
                    if g >= 1:
                        weigh(*order[g - 1], hp)

        @block.scalar
        def _(act):
            for name in ("q_ready", "exps", "copied", "outs"):
                act.sem_inc(s(name), 1)
            with act.Fori(0, HEADS // 2) as hp:
                for j in range(2):
                    act.wait_ge(s("scores"), nth(0, hp))
                    settle(act, s("settled_act"))
                    act.copy(qh[0:QK, j, :], m.qT[0:QK, bass.ds(2 * hp + j, 1), :].squeeze(1))\
                       .then_inc(s("q_ready"), 1)

                def exps(g):
                    c, n, ks = ITEMS[g % NI]
                    nk = keys_of(ITEMS[g % NI])
                    b = 2 * (g % 2)
                    act.wait_ge(s("negmax"), nth(g + 1, hp))
                    act.wait_ge(s("turned"), nth(max(g - 1, 0), hp))
                    act.activation(pr[0:n, g % 2, 0:nk], m.ps[0:n, b:b + 2, :].rearrange("p b c -> p (b c)")[:, 0:nk],
                                   ACT.Exp, bias=mx[0:n, 2 + g % 2:3 + g % 2], scale=ATT_SCALE,
                                   accum_out=sm[0:n, g % 2:g % 2 + 1]).then_inc(s("exps"), 1)

                def outs(g):
                    c, n, _ = ITEMS[g % NI]
                    j = g // NI
                    r = slice(j * V_DIM, (j + 1) * V_DIM)
                    act.wait_ge(s("weighed"), nth(g + 1, hp))
                    settle(act, s("settled_act"))
                    act.copy(m.qT[r, bass.ds(2 * hp, 1), c:c + n].squeeze(1), m.ps[r, 6 + g % 2, 0:n])\
                       .then_inc(s("outs"), 1)

                def copies(g):
                    c, n, ks = ITEMS[g % NI]
                    full = [k for k in ks if k[2] == P]
                    act.wait_ge(s("turned"), nth(g + 1, hp))
                    act.wait_ge(s("weighed"), nth(max(g - 1, 0), hp))
                    src = m.ps[:, 4:6, :].rearrange("p b (u c) -> p (b u) c", c=P)
                    dst = pt[:, g % 2, :].rearrange("p (u c) -> p u c", c=P)
                    ins = act.copy(dst[:, 0:len(full), 0:n], src[:, 0:len(full), 0:n])
                    if len(full) < len(ks):
                        kn = ks[-1][2]
                        ins = act.copy(dst[0:kn, len(full), 0:n], src[0:kn, len(full), 0:n])
                    ins.then_inc(s("copied"), 1)

                for g in range(HI + 2):
                    if g < HI:
                        exps(g)
                    if 1 <= g <= HI:
                        copies(g - 1)
                    if g >= 2:
                        outs(g - 2)

        @block.vector
        def _(dve):
            for name in ("v_ready", "masked", "max", "negmax", "rsum", "probs"):
                dve.sem_inc(s(name), 1)
            with dve.Fori(0, HEADS // 2) as hp:
                for j in range(2):
                    dve.wait_ge(s("weighed"), nth(0, hp))
                    dve.tensor_copy(vh[:, j, :, :], m.V[:, :, bass.ds((2 * hp + j) * V_DIM, V_DIM)])\
                       .then_inc(s("v_ready"), 1)

                def maximum(g):
                    c, n, ks = ITEMS[g % NI]
                    nk = keys_of(ITEMS[g % NI])
                    b = 2 * (g % 2)
                    sc = m.ps[0:n, b:b + 2, :].rearrange("p b c -> p (b c)")[:, 0:nk]
                    dve.wait_ge(s("scores"), nth(g + 1, hp))
                    if n == P:
                        dve.memset(sc[0:CH, nk - CH:nk], NEG).then_inc(s("masked"), 1)
                        dve.wait_ge(s("masked"), at(g - g // NI + 2, HI - 2, hp))
                    dve.tensor_reduce(mx[0:n, g % 2:g % 2 + 1], sc, AX_X, ALU.max).then_inc(s("max"), 1)
                    dve.wait_ge(s("max"), nth(g + 1, hp))
                    dve.wait_ge(s("exps"), nth(max(g - 1, 0), hp))
                    dve.tensor_scalar(mx[0:n, 2 + g % 2:3 + g % 2], mx[0:n, g % 2:g % 2 + 1], -ATT_SCALE, None,
                                      ALU.mult).then_inc(s("negmax"), 1)

                def normalise(g):
                    c, n, ks = ITEMS[g % NI]
                    nk = keys_of(ITEMS[g % NI])
                    dve.wait_ge(s("exps"), nth(g + 1, hp))
                    dve.reciprocal(sm[0:n, 2 + g % 2:3 + g % 2], sm[0:n, g % 2:g % 2 + 1]).then_inc(s("rsum"), 1)
                    dve.wait_ge(s("rsum"), nth(g + 1, hp))
                    dve.tensor_scalar(pr[0:n, g % 2, 0:nk], pr[0:n, g % 2, 0:nk], sm[0:n, 2 + g % 2:3 + g % 2],
                                      None, ALU.mult).then_inc(s("probs"), 1)

                maximum(0)
                for g in range(HI):
                    normalise(g)
                    if g + 1 < HI:
                        maximum(g + 1)

    s = Sems(nc, m.limbo, "mix")
    with ExitStack() as mem:
        mem.callback(s.close)
        block = mem.enter_context(nc.Block())
        KA = HEADS // 2

        @block.gpsimd
        def _(pool):
            for k in range(KA):
                pool.memset(m.qT[:, 2 * k, SEQ:S0], 0.0).then_inc(s("gap"), 1)

        @block.scalar
        def _(act):
            act.wait_ge(s("gap"), KA)
            for k in range(KA):
                act.copy(m.xhi[:, 2 * k + 1, :], m.qT[:, 2 * k, :]).then_inc(s("hi"), 1)
            for k in range(KA):
                act.wait_ge(s("lo"), k + 1)
                act.copy(m.xhi[:, 2 * k, :], m.osc[:, k, :]).then_inc(s("hi"), 1)

        @block.vector
        def _(dve):
            for k in range(KA):
                dve.wait_ge(s("hi"), k + 1)
                dve.tensor_tensor(m.xlo[:, 2 * k + 1, :], m.qT[:, 2 * k, :], m.xhi[:, 2 * k + 1, :].bitcast(F32),
                                  ALU.subtract).then_inc(s("lo"), 1)
            for k in range(KA):
                dve.wait_ge(s("hi"), KA + k + 1)
                dve.tensor_tensor(m.xlo[:, 2 * k, :], m.osc[:, k, :], m.xhi[:, 2 * k, :].bitcast(F32),
                                  ALU.subtract).then_inc(s("lo"), 1)



def out_block(nc, ctx, m, d, name, w, slots):
    s = Sems(nc, m.limbo, name)
    m.raws = 2
    RING = 4
    with ExitStack() as mem:
        mem.callback(s.close)
        block = mem.enter_context(nc.Block())

        @block.sync
        def _(sp):
            sp.dma_start(m.z[:, :, :].rearrange("p k t -> p (k t)"), d["residual"]).then_inc(s("z_in"), 16)
            for j in range(KD):
                load_unit(sp, m, s, 0, j, 0, None, column_unit(w, j * P), UNIT)

        @block.gpsimd
        def _(pool):
            for j in range(KD):
                split_unit(pool, m, s, 0, j, 0, None, RING, UNIT)

        @block.tensor
        def _(pe):
            for j in range(KD):
                tile_product(pe, m, s, j, 0, None, RING, j % 2, j // 2, 0, slots, done=min(j, 1))

        @block.vector
        def _(dve):
            dve.wait_ge(s("z_in"), 16)
            for j in range(KD):
                g = j % 2
                for q, cols in enumerate(SPLIT):
                    dve.wait_ge(s(f"full{g}"), SPL * (j // 2) + q + 1)
                    dve.tensor_tensor(m.z[:, j, cols], m.ps[:, 3 * g + q, 0:NS], m.z[:, j, cols], ALU.add)\
                       .then_inc(s(f"free{g}"), 1)



def ffn_block(nc, ctx, m, d, layer):
    s = Sems(nc, m.limbo, f"ff{layer}")
    m.raws = 3
    RING = 4
    CT = 2
    NCH = FT // CT
    LOOPS = (NCH - 1) // 2
    w_in, w_out = d["w_ff_in"][layer], d["w_ff_out"][layer]
    FFW = f"ffw{layer}"
    U0, UL = 2 * CT, 2 * 3 * CT
    with ExitStack() as mem:
        mem.callback(s.close)
        hhi = mem.enter_context(nc.sbuf_tensor(f"ff{layer}_hhi", [P, 2, CT, TW], F32R))
        hlo = mem.enter_context(nc.sbuf_tensor(f"ff{layer}_hlo", [P, 2, CT, TW], F32R))
        gb = mem.enter_context(nc.sbuf_tensor(f"ff{layer}_gate", [P, GAP + TW], F32))
        cv = mem.enter_context(nc.sbuf_tensor(f"ff{layer}_conv", [P, TW], F32))
        sg = mem.enter_context(nc.sbuf_tensor(f"ff{layer}_sig", [P, TW], F32))
        st = mem.enter_context(nc.sbuf_tensor(f"ff{layer}_st", [P, 4, FT], F32))
        block = mem.enter_context(nc.Block())

        @block.sync
        def _(sp):
            def load_in(base, per, i, f):
                for k in range(CT):
                    load_unit(sp, m, s, base, 2 * k, per, i, column_unit(w_in, (f + k) * P), UNIT)
                    load_unit(sp, m, s, base, 2 * k + 1, per, i, column_unit(w_in, (f + k) * P + F), UNIT)

            def load_out(base, per, i, f):
                for k in range(CT):
                    load_unit(sp, m, s, base, k, per, i, w_out[bass.ds((f + k) * P, P), :], UNIT)

            load_in(0, 0, None, 0)
            with sp.Fori(0, LOOPS) as i:
                load_in(U0, UL, i, (2 * i + 1) * CT)
                load_out(U0 + 4, UL, i, 2 * i * CT)
                load_in(U0 + 6, UL, i, (2 * i + 2) * CT)
                load_out(U0 + 10, UL, i, (2 * i + 1) * CT)
            load_out(U0 + UL * LOOPS, 0, None, (NCH - 1) * CT)
            sp.wait_ge(s("st_rows"), 1)
            for r in range(4):
                dst = d["p_ffconv"] if r < 2 else d["s_ffconv"]
                sp.dma_start(dst[layer, 0, r % 2].rearrange("(t p) -> t p", p=P), m.strow[r * FT:(r + 1) * FT, :])\
                  .then_inc(s("st_out"), 16)
            sp.wait_ge(s("st_out"), 64)

        @block.gpsimd
        def _(pool):
            pool.memset(gb[:, 0:GAP], 0.0).then_inc(s("past0"), 1)
            for j in range(U0):
                split_unit(pool, m, s, 0, j, 0, None, RING, UNIT)
            with pool.Fori(0, LOOPS) as i:
                for j in range(UL):
                    split_unit(pool, m, s, U0, j, UL, i, RING, UNIT)
            for j in range(2):
                split_unit(pool, m, s, U0 + UL * LOOPS, j, 0, None, RING, UNIT)

        @block.tensor
        def _(pe):
            def products(base, per, i, c0, done):
                for k in range(CT):
                    for g in range(2):
                        tile_product(pe, m, s, base + 2 * k + g, per, i, RING, g, c0 * CT + k, 2 * CT,
                                     range(KD), done=done if k + g == 0 else 1)

            def outs(base, per, i, c0):
                b = c0 % 2
                pe.wait_ge(s("w_lo"), at(base + 2, per, i))
                pe.wait_ge(s("h_lo"), at(CT * (c0 + 1), 2 * CT, i))
                for o in range(KD):
                    for q in range(SPL):
                        n = SPL * o + q
                        seq = SPL * KD * c0 + n
                        if seq >= 2:
                            pe.wait_ge(s("out_free"), at(seq - 1, 2 * SPL * KD, i))
                        for k in range(CT):
                            r = (base + k) % RING
                            w = slice(o * P, (o + 1) * P)
                            ins = mm3(pe, m.ps[:, 6 + seq % 2, 0:NS], m.whi[:, r, w], m.wlo[:, r, w],
                                      hhi[:, b, k, SPLIT[q]], hlo[:, b, k, SPLIT[q]], k == 0, k == CT - 1,
                                      s, 1 if n == 0 and k == 0 else 0)
                        ins.then_inc(s("out_full"), 1)

            products(0, 0, None, 0, 0)
            pe.sem_inc(s("out_some"), 1)
            with pe.Fori(0, LOOPS) as i:
                products(U0, UL, i, 1, 1)
                outs(U0 + 4, UL, i, 0)
                products(U0 + 6, UL, i, 2, 2)
                outs(U0 + 10, UL, i, 1)
                pe.wait_ge(s("out_full"), 2 * SPL * KD * (i + 1))
                pe.sem_inc(s("w_used"), 1)
                pe.sem_inc(s("out_some"), 1)
            outs(U0 + UL * LOOPS, 0, None, NCH - 1)
            pe.wait_ge(s("st_done"), FT)
            pe.transpose(m.ps[0:4 * FT, 0, 0:P], st[:, :, :].rearrange("p r t -> p (r t)"), m.ident[:, :])\
              .then_inc(s("st_turned"), 1)

        def act_chunk(act, i, c0):
            for k in range(CT):
                t = c0 * CT + k
                for q in range(SPL):
                    act.wait_ge(s("full0"), at(SPL * t + q + 1, SPL * 2 * CT, i))
                    if q == 0 and t >= 1:
                        act.wait_ge(s("conv"), at(3 * t, 6 * CT, i))
                        act.wait_ge(s("st_done"), at(t, 2 * CT, i))
                    act.copy(gb[:, GAP + q * NS:GAP + (q + 1) * NS], m.ps[:, q, 0:NS]).then_inc(s("free0"), 1)
                act.wait_ge(s("conv"), at(3 * (t + 1), 6 * CT, i))
                if t >= 1:
                    act.wait_ge(s("silu"), at(t, 2 * CT, i))
                act.activation(sg[:, :], cv[:, :], ACT.Sigmoid).then_inc(s("sig"), 1)
                act.wait_ge(s("h"), at(t + 1, 2 * CT, i))
                if c0 >= 2:
                    act.wait_ge(s("out_full"), at(SPL * KD * (c0 - 1), 2 * SPL * KD, i))
                elif c0 == 1 and k == 0:
                    act.wait_ge(s("out_some"), i + 1)
                act.copy(hhi[:, c0 % 2, k, :], cv[:, :]).then_inc(s("h_hi"), 1)

        @block.scalar
        def _(act):
            act_chunk(act, None, 0)
            with act.Fori(0, LOOPS) as i:
                act_chunk(act, i, 1)
                act_chunk(act, i, 2)

        def dve_chunk(dve, i, c0):
            for k in range(CT):
                t = c0 * CT + k
                tt = at(t, 2 * CT, i)
                one = lambda name, j: m.par[:, bass.ds(tt + pcol(name, j), 1)]
                dve.wait_ge(s("free0"), at(SPL * (t + 1), SPL * 2 * CT, i))
                for r in range(2):
                    dve.tensor_copy(st[:, r, bass.ds(tt, 1)], gb[:, GAP + SEQ - 2 + r:GAP + SEQ - 1 + r])
                    ins = dve.tensor_copy(st[:, 2 + r, bass.ds(tt, 1)], gb[:, GAP + TW - 2 + r:GAP + TW - 1 + r])
                    dve.tensor_copy(gb[:, GAP + S0 - 2 + r:GAP + S0 - 1 + r],
                                    one("ffstate", layer * 2 * FT + r * FT)).then_inc(s("past"), 1)
                ins.then_inc(s("st_done"), 1)
                dve.wait_ge(s("past"), at(2 * (t + 1), 4 * CT, i))
                dve.wait_ge(s("past0"), 1)
                if t >= 1:
                    dve.wait_ge(s("h_lo"), at(t, 2 * CT, i))
                dve.tensor_scalar(cv[:, :], gb[:, 2:2 + TW], one(FFW, 0), None, ALU.mult).then_inc(s("conv"), 1)
                for kk in (1, 2):
                    dve.wait_ge(s("conv"), at(3 * t + kk, 6 * CT, i))
                    dve.scalar_tensor_tensor(cv[:, :], gb[:, 2 + kk:2 + kk + TW], one(FFW, FT * kk), cv[:, :],
                                             ALU.mult, ALU.add).then_inc(s("conv"), 1)
                dve.wait_ge(s("sig"), at(t + 1, 2 * CT, i))
                dve.tensor_tensor(cv[:, :], cv[:, :], sg[:, :], ALU.mult).then_inc(s("silu"), 1)
                dve.wait_ge(s("silu"), at(t + 1, 2 * CT, i))
                for q in range(SPL):
                    dve.wait_ge(s("full1"), at(SPL * t + q + 1, SPL * 2 * CT, i))
                    dve.tensor_tensor(cv[:, SPLIT[q]], m.ps[:, 3 + q, 0:NS], cv[:, SPLIT[q]], ALU.mult)\
                       .then_inc(s("free1"), 1)
                dve.wait_ge(s("free1"), at(SPL * (t + 1), SPL * 2 * CT, i))
                dve.nop().then_inc(s("h"), 1)
                dve.wait_ge(s("h_hi"), at(t + 1, 2 * CT, i))
                dve.tensor_tensor(hlo[:, c0 % 2, k, :], cv[:, :], hhi[:, c0 % 2, k, :].bitcast(F32),
                                  ALU.subtract).then_inc(s("h_lo"), 1)

        def dve_outs(dve, i, c0):
            for n in range(SPL * KD):
                o, q = n // SPL, n % SPL
                seq = SPL * KD * c0 + n
                dve.wait_ge(s("out_full"), at(seq + 1, 2 * SPL * KD, i))
                dve.tensor_tensor(m.z[:, o, SPLIT[q]], m.ps[:, 6 + seq % 2, 0:NS], m.z[:, o, SPLIT[q]], ALU.add)\
                   .then_inc(s("out_free"), 1)

        @block.vector
        def _(dve):
            dve_chunk(dve, None, 0)
            with dve.Fori(0, LOOPS) as i:
                dve_chunk(dve, i, 1)
                dve_outs(dve, i, 0)
                dve_chunk(dve, i, 2)
                dve_outs(dve, i, 1)
            dve_outs(dve, None, NCH - 1)
            dve.wait_ge(s("st_turned"), 1)
            dve.tensor_copy(m.strow[0:4 * FT, :], m.ps[0:4 * FT, 0, 0:P]).then_inc(s("st_rows"), 1)



def odd_in_block(nc, ctx, m, d):
    s = Sems(nc, m.limbo, "oin")
    w = d["w_in_o"][0]
    m.raws = 2
    RING = 4
    KT = 3 * HEADS
    with ExitStack() as mem:
        mem.callback(s.close)
        sb = lambda n, shape: mem.enter_context(nc.sbuf_tensor("oin_" + n, shape, F32))
        raw = sb("raw", [P, 3, GAP + TW])
        zb = sb("z", [P, TW])
        cv = sb("conv", [P, TW])
        sg = sb("sig", [P, TW])
        ob = sb("out", [P, 4, TW])
        st = sb("st", [P, 2, 3, KT])
        strow = sb("strow", [3 * KT, 2, P])
        block = mem.enter_context(nc.Block())

        @block.sync
        def _(sp):
            load_unit(sp, m, s, 0, 0, 0, None, column_unit(w, 4 * DN_KEY, 16), KD * 16)
            for j in range(3):
                load_unit(sp, m, s, 0, j + 1, 0, None, column_unit(w, j * DN_KEY), UNIT)

            def stores(h):
                for k in range(4):
                    sp.wait_ge(s(f"tile{k}"), h + 1)
                    sp.dma_start(d["qkvz"][k, bass.ds(h, 1)].squeeze(0), ob[:, k, :]).then_inc(s(f"stored{k}"), 16)

            with sp.Fori(0, HEADS - 1) as h:
                load_unit(sp, m, s, 4, 0, 4, h, column_unit(w, h * P + 3 * DN_KEY), UNIT)
                for j in range(3):
                    load_unit(sp, m, s, 4, j + 1, 4, h, column_unit(w, h * P + j * DN_KEY + P), UNIT)
                stores(h)
            load_unit(sp, m, s, 4 * HEADS, 0, 0, None, column_unit(w, (HEADS - 1) * P + 3 * DN_KEY), UNIT)
            stores(HEADS - 1)
            sp.wait_ge(s("gates"), 1)
            sp.dma_start(m.bt[:, :], m.ab[HEADS:2 * HEADS, :]).then_inc(s("bt"), 16)
            sp.wait_ge(s("st_rows"), 1)
            for k, name in enumerate(("p_dconv", "s_dconv")):
                sp.dma_start(d[name][0, 0].rearrange("r (t p) -> (r t) p", p=P), strow[:, k, :])\
                  .then_inc(s("st_out"), 16)
            sp.wait_ge(s("st_out"), 32)
            sp.wait_ge(s("bt"), 16)
            for k in range(4):
                sp.wait_ge(s(f"stored{k}"), 16 * HEADS + 1)

        @block.gpsimd
        def _(pool):
            pool.memset(raw[:, :, 0:GAP], 0.0).then_inc(s("past0"), 1)
            split_unit(pool, m, s, 0, 0, 0, None, RING, KD * 16)
            for j in range(1, 4):
                split_unit(pool, m, s, 0, j, 0, None, RING, UNIT)
            with pool.Fori(0, HEADS - 1) as h:
                for j in range(4):
                    split_unit(pool, m, s, 4, j, 4, h, RING, UNIT)
            split_unit(pool, m, s, 4 * HEADS, 0, 0, None, RING, UNIT)

        @block.tensor
        def _(pe):
            tile_product(pe, m, s, 0, 0, None, RING, 1, 0, 0, range(KD), done=0, cols=16)
            tile_product(pe, m, s, 1, 0, None, RING, 0, 0, 0, range(KD))
            tile_product(pe, m, s, 2, 0, None, RING, 1, 1, 0, range(KD))
            tile_product(pe, m, s, 3, 0, None, RING, 0, 1, 0, range(KD))
            with pe.Fori(0, HEADS - 1) as h:
                tile_product(pe, m, s, 4, 4, h, RING, 1, 2, 2, range(KD))
                tile_product(pe, m, s, 5, 4, h, RING, 0, 2, 2, range(KD))
                tile_product(pe, m, s, 6, 4, h, RING, 1, 3, 2, range(KD))
                tile_product(pe, m, s, 7, 4, h, RING, 0, 3, 2, range(KD))
            tile_product(pe, m, s, 4 * HEADS, 0, None, RING, 1, 2 * HEADS, 0, range(KD))
            pe.wait_ge(s("st_done"), KT + 1)
            for k in range(2):
                ins = pe.transpose(m.ps[0:3 * KT, 6 + k, 0:P], st[:, k, :, :].rearrange("p r t -> p (r t)"),
                                   m.ident[:, :])
            ins.then_inc(s("st_turned"), 1)

        @block.scalar
        def _(act):
            with act.Fori(0, HEADS) as h:
                for k, j in ((0, 0), (2, 1)):
                    act.wait_ge(s("st_done"), 3 * h + 1)
                    for q in range(SPL):
                        act.wait_ge(s("full0"), at(SPL * j + q + 1, 2 * SPL, h))
                        act.copy(raw[:, k, GAP + q * NS:GAP + (q + 1) * NS], m.ps[:, q, 0:NS])\
                           .then_inc(s("free0"), 1)
                    if k == 0:
                        sigmoids = (0, 1)
                    else:
                        sigmoids = (2, 3)
                    for n in sigmoids:
                        act.wait_ge(s("conv"), at(n + 1, 4, h))
                        act.activation(sg[:, :], (zb if n == 3 else cv)[:, :], ACT.Sigmoid).then_inc(s("sig"), 1)

        @block.vector
        def _(dve):
            dve.sem_inc(s("st_done"), 1)
            for k in range(4):
                dve.sem_inc(s(f"stored{k}"), 1)
            for q in range(SPL):
                dve.wait_ge(s("full1"), q + 1)
                dve.tensor_copy(m.ab[:, SPLIT[q]], m.ps[0:16, 3 + q, 0:NS]).then_inc(s("free1"), 1)
            dve.wait_ge(s("free1"), SPL)
            dve.sem_inc(s("gates"), 1)
            dve.wait_ge(s("past0"), 1)
            with dve.Fori(0, HEADS) as h:
                for k in range(4):
                    if k in (0, 2):
                        dve.wait_ge(s("free0"), at(SPL * (k // 2 + 1), 2 * SPL, h))
                    for q in range(SPL):
                        if k in (1, 3):
                            n1 = SPL * (1 + k // 2) + q + 1
                            dve.wait_ge(s("full1"), at(n1, 2 * SPL, h))
                            dst = raw[:, 1, GAP + q * NS:GAP + (q + 1) * NS] if k == 1 else zb[:, SPLIT[q]]
                            ins = dve.tensor_copy(dst, m.ps[:, 3 + q, 0:NS])
                            ins.then_inc(s("free1"), 1)
                    if k in (1, 3):
                        dve.wait_ge(s("free1"), at(SPL * (2 + k // 2), 2 * SPL, h))
                    if k < 3:
                        x = raw[:, k, :]
                        one = lambda name, r: m.par[:, bass.ds(h + pcol(name, r * KT + k * HEADS), 1)]
                        for r in range(3):
                            dve.tensor_copy(st[:, 0, r, bass.ds(h + k * HEADS, 1)],
                                            x[:, GAP + SEQ - 3 + r:GAP + SEQ - 2 + r])
                            dve.tensor_copy(st[:, 1, r, bass.ds(h + k * HEADS, 1)],
                                            x[:, GAP + TW - 3 + r:GAP + TW - 2 + r])
                            dve.tensor_copy(x[:, GAP + S0 - 3 + r:GAP + S0 - 2 + r], one("dstate", r))\
                               .then_inc(s("past"), 1)
                        dve.wait_ge(s("past"), at(3 * (k + 1), 9, h))
                        dve.tensor_scalar(cv[:, :], x[:, 1:1 + TW], one("dconv", 0), None, ALU.mult)\
                           .then_inc(s("taps"), 1)
                        for t in (1, 2, 3):
                            dve.wait_ge(s("taps"), at(4 * k + t, 12, h))
                            dve.scalar_tensor_tensor(cv[:, :], x[:, 1 + t:1 + t + TW], one("dconv", t), cv[:, :],
                                                     ALU.mult, ALU.add).then_inc(s("taps"), 1)
                        dve.wait_ge(s("taps"), at(4 * (k + 1), 12, h))
                        dve.sem_inc(s("st_done"), 1)
                    dve.sem_inc(s("conv"), 1)
                    dve.wait_ge(s("sig"), at(k + 1, 4, h))
                    dve.wait_ge(s(f"stored{k}"), 16 * h + 1)
                    dve.tensor_tensor(ob[:, k, :], (zb if k == 3 else cv)[:, :], sg[:, :], ALU.mult)\
                       .then_inc(s(f"tile{k}"), 1)
                    dve.wait_ge(s(f"tile{k}"), h + 1)
            dve.wait_ge(s("st_turned"), 1)
            for k in range(2):
                ins = dve.tensor_copy(strow[:, k, :], m.ps[0:3 * KT, 6 + k, 0:P])
            ins.then_inc(s("st_rows"), 1)



LEVELS = 6
NCHUNK = SEQ // CH + DEC // CH


def gates_block(nc, ctx, m, d):
    s = Sems(nc, m.limbo, "gate")
    with ExitStack() as mem:
        mem.callback(s.close)
        sb = lambda n, shape: mem.enter_context(nc.sbuf_tensor("gate_" + n, shape, F32))
        t0 = sb("t0", [HEADS, TW])
        t1 = sb("t1", [HEADS, TW])
        keep = sb("keep", [HEADS, TW])
        nega = sb("nega", [HEADS, 8])
        block = mem.enter_context(nc.Block())

        @block.sync
        def _(sp):
            for k, (rows, name) in enumerate(((m.G, "G"), (m.beta, "beta"))):
                sp.wait_ge(s(name), 1)
                sp.dma_start(d["gates"][0:NPAIR * 2, k].rearrange("n h c -> h n c"),
                             rows[:, 0:SEQ].rearrange("h (n c) -> h n c", c=CH)).then_inc(s("out"), 16)
                sp.dma_start(d["gates"][2 * NPAIR, k], rows[:, S0:S0 + DEC]).then_inc(s("out"), 16)
            sp.wait_ge(s("out"), 64)

        @block.gpsimd
        def _(pool):
            n = 0

            def step(ins):
                nonlocal n
                n += 1
                ins.then_inc(s("step"), 1)
                pool.wait_ge(s("step"), n)

            step(pool.memset(keep[:, :], 1.0))
            step(pool.memset(keep[:, 0:SEQ].rearrange("h (c t) -> h c t", t=CH)[:, :, 0:1], 0.0))
            step(pool.memset(keep[:, S0:S0 + 1], 0.0))
            pool.sem_inc(s("keep"), 1)
            step(pool.memset(m.masks[:, :, :], 0.0))
            step(pool.memset(m.levt[:, :, :], 0.0))
            for b in range(2):
                rows = slice(CH * b, CH * (b + 1))

                def select(v, cond, base, pattern, ch, fill=0.0):
                    step(pool.affine_select(out=v, in_=v, compare_op=cond, fill=fill, base=base,
                                            pattern=pattern, channel_multiplier=ch))

                select(m.masks[rows, m.EYE, :], ALU.not_equal, 0, [[-1, CH]], 1, 1.0)
                step(pool.memset(m.masks[rows, m.UPI:m.UPS + 1, :], 1.0))
                select(m.masks[rows, m.UPI, :], ALU.is_ge, 0, [[1, CH]], -1)
                select(m.masks[rows, m.UPS, :], ALU.is_gt, 0, [[1, CH]], -1)
                for low, l in [(True, 0)] + [(False, l) for l in range(LEVELS)]:
                    z = 2 << l
                    if l >= 1:
                        v = m.levt[rows, l - 1, :]
                    else:
                        v = m.masks[rows, m.LEV if low else m.LEVT, :]
                    v = v.rearrange("p (n h c) -> p n h c", h=2, c=z // 2)
                    v = v[:, :, 0 if low else 1, :]
                    lo = z // 2 if low else 0
                    step(pool.memset(v, -1.0 if l == 0 else 1.0))
                    select(v, ALU.is_ge, -lo, [[-z, CH // z], [0, z // 2]], 1)
                    select(v, ALU.is_ge, lo + z // 2 - 1, [[z, CH // z], [0, z // 2]], -1)

        @block.scalar
        def _(act):
            act.activation(m.beta[:, :], m.bt[:, :], ACT.Sigmoid).then_inc(s("beta"), 1)
            act.activation(t0[:, :], m.ab[0:HEADS, :], ACT.Abs, bias=m.dtb).then_inc(s("abs"), 1)
            act.activation(nega[:, 0:1], m.alog, ACT.Exp).then_inc(s("ea"), 1)
            act.wait_ge(s("abs"), 1)
            act.activation(t0[:, :], t0[:, :], ACT.Exp, scale=-1.0).then_inc(s("e"), 1)
            act.wait_ge(s("e"), 1)
            act.activation(t0[:, :], t0[:, :], ACT.Ln, bias=m.ones[0:HEADS, 0:1]).then_inc(s("ln"), 1)
            act.wait_ge(s("gcol"), 1)
            act.activation(m.bcol[:, :, :], m.gcol[:, :, 0:HEADS], ACT.Exp).then_inc(s("egcol"), 1)

        @block.vector
        def _(dve):
            dve.tensor_scalar(t1[:, :], m.ab[0:HEADS, :], m.dtb, 0.0, ALU.add, ALU.max).then_inc(s("relu"), 1)
            dve.wait_ge(s("ln"), 1)
            dve.wait_ge(s("relu"), 1)
            dve.tensor_tensor(t1[:, :], t1[:, :], t0[:, :], ALU.add).then_inc(s("sp"), 1)
            dve.wait_ge(s("ea"), 1)
            dve.tensor_scalar(nega[:, 1:2], nega[:, 0:1], -1.0, None, ALU.mult).then_inc(s("na"), 1)
            dve.wait_ge(s("sp"), 1)
            dve.wait_ge(s("na"), 1)
            dve.tensor_scalar(t1[:, :], t1[:, :], nega[:, 1:2], None, ALU.mult).then_inc(s("g"), 1)
            dve.wait_ge(s("g"), 1)
            dve.wait_ge(s("keep"), 1)
            dve.tensor_tensor_scan(m.G[:, :], keep[:, :], t1[:, :], 0.0, ALU.mult, ALU.add).then_inc(s("G"), 1)
            dve.memset(m.gcol[:, :, :], 0.0).then_inc(s("gzero"), 1)
            dve.wait_ge(s("gzero"), 1)
            dve.wait_ge(s("turned"), 1)
            turned = m.ps[:, 0, 0:9 * 16].rearrange("p (t c) -> p t c", c=16)
            dve.tensor_copy(m.gcol[:, 0:8, :], turned[:, 0:8, :])
            dve.tensor_copy(m.gcol[0:DEC, 8, :], turned[0:DEC, 8, :]).then_inc(s("gcol"), 1)
            dve.wait_ge(s("egcol"), 1)
            dve.tensor_tensor(m.bcol[:, :, :], m.bcol[:, :, :], m.gcol[:, :, HEADS:2 * HEADS], ALU.mult)
            dve.tensor_scalar(m.go[:, 0:1], m.par[:, pcol("go", 0):pcol("go", 0) + 1], DK ** 0.5, None, ALU.mult)

        @block.tensor
        def _(pe):
            pe.wait_ge(s("G"), 1)
            pe.wait_ge(s("beta"), 1)
            for t in range(9):
                c, n = TILES[t]
                pe.transpose(m.ps[0:n, 0, t * 16:t * 16 + 8], m.G[:, c:c + n], m.ident[0:HEADS, 0:HEADS])
                ins = pe.transpose(m.ps[0:n, 0, t * 16 + 8:t * 16 + 16], m.beta[:, c:c + n],
                                   m.ident[0:HEADS, 0:HEADS])
            ins.then_inc(s("turned"), 1)



class Pair:

    def __init__(self, k, i=None):
        self.k, self.i = k, i
        self.n = DEC if k == NPAIR else P
        self.odd = k % 2
        self.index = at(k, 2, i)
        self.col = S0 if k == NPAIR else at(k * P, 2 * P, i)
        self.first = i is None and k == 0

    def blocks(self):
        return [slice(CH * b, CH * (b + 1)) for b in range(self.n // CH)]

    def th(self, a, per):
        return at(a + per * self.k, 2 * per, self.i)


def delta_block(nc, ctx, m, d):
    s = Sems(nc, m.limbo, "dn")
    H, L = HEADS, CH
    GR = H // 2
    HALVES = (slice(0, GR), slice(GR, H))
    with ExitStack() as mem:
        mem.callback(s.close)
        sb = lambda n, shape: mem.enter_context(nc.sbuf_tensor("dn_" + n, shape, F32))
        (ML, T, TT, X, MT, AT0, AT1, low, upi, ups, upl) = m.delta_small
        kq = (sb("q0", [P, H, P]), sb("q1", [P, H, P]))
        kk, kv, kz, sq, qs, rt = (sb(n, [P, H, P]) for n in ("k", "v", "z", "sq", "qs", "rt"))
        eg = sb("eg", [P, 2, H, L])
        GB = sb("gb", [P, 2, H, L])
        AT = (AT0, AT1)
        kbg, vb, kc, vn, Sg = (sb(n, [P, H, P]) for n in ("kbg", "vb", "kc", "vn", "Sg"))
        ktl = (sb("ktl0", [P, H, P]), sb("ktl1", [P, H, P]))
        S = (sb("S0", [P, H, P]), sb("S1", [P, H, P]))
        egl = sb("egl", [P, 2, 2, H])
        block = mem.enter_context(nc.Block())

        def bank2(b, n=P):
            return m.ps[:, b:b + 2, :].rearrange("p b (h c) -> p (b h) c", c=P)[:, :, 0:n]

        def bank1(b):
            return m.ps[:, b, :].rearrange("p (h c) -> p h c", c=L)

        def masked(k, n):
            return m.masks[0:n, k, :].unsqueeze(1).to_broadcast([n, H, L])

        def stages(engine, run):
            run(Pair(0), None, Pair(1))
            with engine.Fori(0, NPAIR // 2 - 1) as i:
                run(Pair(1, i), Pair(0, i), Pair(2, i))
                run(Pair(2, i), Pair(1, i), Pair(3, i))
            run(Pair(NPAIR - 1), Pair(NPAIR - 2), Pair(NPAIR))
            run(Pair(NPAIR), Pair(NPAIR - 1), None)
            run(None, Pair(NPAIR), None)

        @block.sync
        def _(sp):
            def heads_of(k, p):
                return d["qkvz"][k].rearrange("h p t -> p h t")[:, :, bass.ds(p.col, p.n)]

            def load_gates(p):
                for b, r in enumerate(p.blocks()):
                    src = d["gates"][bass.ds(p.th(b, 2), 1)].squeeze(0).rearrange("k h c -> (k h c)")
                    sp.dma_start(GB[r].rearrange("p k h c -> p (k h c)"),
                                 src.unsqueeze(0).to_broadcast([L, 2 * H * L])).then_inc(s("in_gb"), 16)

            def load_decays(p):
                for b, r in enumerate(p.blocks()):
                    src = d["gates"][bass.ds(p.th(b, 2), 1), 0].squeeze(0).rearrange("h c -> (h c)")
                    sp.dma_start(eg[:, b].rearrange("p h c -> p (h c)"),
                                 src.unsqueeze(0).to_broadcast([P, H * L])).then_inc(s("in_eg"), 16)

            p = Pair(0)
            load_gates(p)
            for k, buf in ((1, kk), (0, kq[0]), (2, kv)):
                sp.dma_start(buf[:, :, 0:P], heads_of(k, p)).then_inc(s(f"in{k}"), 16)
            load_decays(p)

            def run(A, B, C):
                if C:
                    sp.wait_ge(s("ups_b"), A.th(1, 1))
                    settle(sp, s("settled_sp"))
                    sp.wait_ge(s("clip"), A.th(2, 2))
                    settle(sp, s("settled_sp"))
                    load_gates(C)
                    sp.wait_ge(s("vturned"), A.th(1, 1))
                    settle(sp, s("settled_sp"))
                    sp.dma_start(kv[:, :, 0:C.n], heads_of(2, C)).then_inc(s("in2"), 16)
                    sp.wait_ge(s("kturned"), A.th(1, 1))
                    settle(sp, s("settled_sp"))
                    sp.dma_start(kk[:, :, 0:C.n], heads_of(1, C)).then_inc(s("in1"), 16)
                    if B:
                        sp.wait_ge(s("o"), B.th(2, 2))
                    settle(sp, s("settled_sp"))
                    sp.dma_start(kq[C.odd][:, :, 0:C.n], heads_of(0, C)).then_inc(s("in0"), 16)
                    sp.wait_ge(s("qd"), A.th(1, 1))
                    settle(sp, s("settled_sp"))
                    sp.wait_ge(s("egl"), A.th(1, 1))
                    settle(sp, s("settled_sp"))
                    load_decays(C)
                if A:
                    if B:
                        sp.wait_ge(s("ofull"), B.th(1, 1))
                    settle(sp, s("settled_sp"))
                    sp.dma_start(kz[:, :, 0:A.n], heads_of(3, A)).then_inc(s("in3"), 16)
                if B and B.k == NPAIR - 1:
                    sp.wait_ge(s("S"), 2 * NPAIR + 1)
                    sp.dma_start(d["p_delta"][0, 0].rearrange("h k v -> k h v"), S[0][:, :, :]).then_inc(s("S_out"), 16)
                    sp.wait_ge(s("S_out"), 16)
                    sp.dma_start(S[0][:, :, :], d["state_delta"][0, 0].rearrange("h k v -> k h v")).then_inc(s("S_in"), 16)

            stages(sp, run)
            sp.wait_ge(s("S"), 2 * NPAIR + 2)
            sp.dma_start(d["s_delta"][0, 0].rearrange("h k v -> k h v"), S[1][:, :, :]).then_inc(s("S_out"), 16)
            sp.wait_ge(s("S_out"), 32)

        @block.gpsimd
        def _(pool):
            pool.memset(S[0][:, :, :], 0.0).then_inc(s("S"), 1)
            pool.memset(m.eps[:, 1:2], EPS * EPS * DK * DK).then_inc(s("eps"), 1)

            def pre(C):
                n = C.n
                pool.wait_ge(s("dlow"), C.th(1, 1))
                pool.tensor_tensor(low[0:n], low[0:n], masked(m.LEV, n), ALU.mult).then_inc(s("low_m"), 1)
                pool.wait_ge(s("dup"), C.th(1, 1))
                pool.tensor_tensor(ups[0:n], upi[0:n], masked(m.UPS, n), ALU.mult).then_inc(s("ups_m"), 1)
                pool.wait_ge(s("low_m"), C.th(1, 1))
                bt = m.gcol[0:n, bass.ds(C.index, 1), H:2 * H].squeeze(1).unsqueeze(2).to_broadcast([n, H, L])
                pool.tensor_tensor(low[0:n], low[0:n], bt, ALU.mult).then_inc(s("low_b"), 1)
                pool.wait_ge(s("ups_m"), C.th(1, 1))
                pool.tensor_tensor(ups[0:n], ups[0:n], GB[0:n, 1], ALU.mult).then_inc(s("ups_b"), 1)
                pool.tensor_tensor(upi[0:n], upi[0:n], masked(m.UPI, n), ALU.mult).then_inc(s("upi_m"), 1)
                pool.wait_ge(s("ups_b"), C.th(1, 1))
                pool.tensor_tensor(upl[0:n], ups[0:n], masked(m.LEVT, n), ALU.mult).then_inc(s("upl"), 1)

            def levels_of(A, ls):
                for l in ls:
                    pool.wait_ge(s("MT"), A.th(1, 1))
                    pool.tensor_tensor(ML[0:A.n, l - 1], MT[0:A.n],
                                       m.levt[0:A.n, l - 1, :].unsqueeze(1).to_broadcast([A.n, H, L]),
                                       ALU.mult).then_inc(s("ML"), 1)

            def decayed(B, b):
                if B.k == NPAIR:
                    pool.wait_ge(s("S_in"), 16)
                pool.wait_ge(s("S"), B.th(b + 1, 2))
                pool.wait_ge(s("egl"), B.th(1, 1))
                pool.tensor_tensor(Sg[:, :, :], S[b][:, :, :], egl[:, B.odd, b, :].unsqueeze(2).to_broadcast([P, H, P]),
                                   ALU.mult).then_inc(s("Sg"), 1)

            def run(A, B, C):
                if B:
                    decayed(B, 0)
                if A:
                    levels_of(A, (1,))
                if B and B.n == P:
                    decayed(B, 1)
                if A:
                    levels_of(A, (2, 3))
                if B:
                    n = B.n
                    pool.wait_ge(s("osq"), B.th(1, 1))
                    pool.wait_ge(s("qs"), B.th(1, 1))
                    pool.tensor_tensor(sq[:, :, 0:n], sq[:, :, 0:n], qs[:, :, 0:n], ALU.add).then_inc(s("osum_in"), 1)
                if A:
                    levels_of(A, (4, 5))
                    pool.wait_ge(s("gramq"), A.th(1, 1))
                    pool.wait_ge(s("qs"), A.th(1, 1))
                    pool.wait_ge(s("eg"), A.th(1, 1))
                    for b, r in enumerate(A.blocks()):
                        ins = pool.tensor_tensor(kq[A.odd][:, :, r], kq[A.odd][:, :, r], eg[:, b], ALU.mult)
                    ins.then_inc(s("qd"), 1)
                if C:
                    pre(C)
                if B:
                    pool.wait_ge(s("onorm"), B.th(2, 1))
                    pool.wait_ge(s("in3"), B.th(16, 16))
                    pool.tensor_tensor(rt[:, :, 0:n], rt[:, :, 0:n], kz[:, :, 0:n], ALU.mult).then_inc(s("ofull"), 1)
                    pool.wait_ge(s("ohi"), B.th(1, 1))
                    pool.tensor_tensor(m.xlo[:, :, bass.ds(B.col, n)], rt[:, :, 0:n],
                                       m.xhi[:, :, bass.ds(B.col, n)].bitcast(F32), ALU.subtract).then_inc(s("olo"), 1)

            for name in ("onorm", "olo"):
                pool.sem_inc(s(name), 1)
            pre(Pair(0))
            stages(pool, run)

        @block.tensor
        def _(pe):
            def old_values(B, b):
                pe.wait_ge(s("kc"), B.th(1, 1))
                pe.wait_ge(s("Tv"), B.th(1, 1))
                pe.wait_ge(s("S"), B.th(b + 1, 2))
                if B.k == NPAIR:
                    pe.wait_ge(s("S_in"), 16)
                r = B.blocks()[b]
                for h in range(H):
                    ins = pe.matmul(bank2(0)[r, h, :], kc[:, h, r], S[b][:, h, :], start=True, stop=True)
                    if h == GR - 1 or h == H - 1:
                        ins.then_inc(s("kS"), 1)

            def state_step(B, b, A):
                if A:
                    pe.wait_ge(s("vb"), A.th(1, 1))
                r = B.blocks()[b]
                for g, hs in enumerate(HALVES):
                    pe.wait_ge(s("vn"), B.th(2 * b + g + 1, 4))
                    for h in range(hs.start, hs.stop):
                        ins = pe.matmul(bank2(4)[:, h, :], ktl[B.odd][r, h, :], vn[r, h, :], start=True, stop=True)
                ins.then_inc(s("dS"), 1)

            def output(B, b):
                pe.wait_ge(s("qd"), B.th(1, 1))
                pe.wait_ge(s("onorm"), B.th(1, 1))
                r = B.blocks()[b]
                for h in range(H):
                    pe.matmul(bank2(2)[:, h, r], S[b][:, h, :], kq[B.odd][:, h, r], start=True, stop=False)
                    ins = pe.matmul(bank2(2)[:, h, r], vn[r, h, :], AT[B.odd][r, h, :], start=False, stop=True)
                ins.then_inc(s("o"), 1)

            def squares_sum(B):
                pe.wait_ge(s("osum_in"), B.th(1, 1))
                for hs in HALVES:
                    ins = pe.matmul(bank2(0, B.n)[:, hs, :], m.ones[:, :], sq[:, hs, 0:B.n], start=True, stop=True)
                ins.then_inc(s("osum"), 1)

            def gram(A, name, bank, x, y):
                settle(pe, s("settled_pe"))
                for r in A.blocks():
                    for h in range(H):
                        ins = pe.matmul(bank1(bank)[r, h, :], x[:, h, r], y[:, h, r], start=True, stop=True)
                ins.then_inc(s(name), 1)

            def turn(A, bank, x, name):
                settle(pe, s("settled_pe"))
                for h in range(H):
                    ins = pe.transpose(bank2(bank)[0:A.n, h, :], x[:, h, 0:A.n], m.ident[:, :])
                ins.then_inc(s(name), 1)

            def run(A, B, C):
                if A:
                    n = A.n
                    pe.wait_ge(s("sqk"), A.th(1, 1))
                    for hs in HALVES:
                        ins = pe.matmul(bank2(6, n)[:, hs, :], m.ones[:, :], sq[:, hs, 0:n], start=True, stop=True)
                    ins.then_inc(s("ksum"), 1)
                    pe.wait_ge(s("in2"), A.th(16, 16))
                    if not A.first:
                        pe.wait_ge(s("kc"), A.th(0, 1))
                    turn(A, 4, kv, "vturned")
                if B:
                    old_values(B, 0)
                if A:
                    pe.wait_ge(s("kn"), A.th(1, 1))
                    gram(A, "gramk", 6, kk, kk)
                if B:
                    state_step(B, 0, A)
                    output(B, 0)
                if A:
                    pe.wait_ge(s("in0"), A.th(16, 16))
                    gram(A, "gramq", 7, kk, kq[A.odd])
                if B and B.n == P:
                    old_values(B, 1)
                if A:
                    pe.wait_ge(s("MT"), A.th(1, 1))
                    pe.wait_ge(s("Ta"), A.th(2, 2))
                    pe.wait_ge(s("AT"), A.th(1, 1))
                    turn(A, 6, kk, "kturned")
                if B and B.n == P:
                    state_step(B, 1, A)
                    output(B, 1)
                if A:
                    if B:
                        pe.wait_ge(s("S"), B.th(3, 2))
                    else:
                        pe.wait_ge(s("vb"), A.th(1, 1))
                    pe.wait_ge(s("kscaled"), A.th(1, 1))
                    for l in range(1, LEVELS):
                        pe.wait_ge(s("ML"), A.th(l, LEVELS - 1))
                        for g, hs in enumerate(HALVES):
                            pe.wait_ge(s("T"), A.th(2 * (l - 1) + g + 1, 2 * (LEVELS - 1)))
                            settle(pe, s("settled_pe"))
                            for r in A.blocks():
                                for h in range(hs.start, hs.stop):
                                    ins = pe.matmul(bank1(4 + g)[r, h, :], ML[r, l - 1, h, :], T[r, h, :],
                                                    start=True, stop=True)
                            ins.then_inc(s("X"), 1)
                        for g, hs in enumerate(HALVES):
                            pe.wait_ge(s("TT"), A.th(2 * (l - 1) + g + 1, 2 * LEVELS))
                            pe.wait_ge(s("Xs"), A.th(2 * (l - 1) + g + 1, 2 * (LEVELS - 1)))
                            settle(pe, s("settled_pe"))
                            for r in A.blocks():
                                for h in range(hs.start, hs.stop):
                                    if l < LEVELS - 1:
                                        pe.matmul(bank1(6 + g)[r, h - hs.start, :], TT[r, h, :], X[r, h, :],
                                                  start=True, stop=True)
                                    ins = pe.matmul(bank1(6 + g)[r, GR + h - hs.start, :], X[r, h, :], TT[r, h, :],
                                                    start=True, stop=True)
                            ins.then_inc(s("Y"), 1)
                        if B and l == 2:
                            squares_sum(B)
                    pe.wait_ge(s("TT"), A.th(2 * LEVELS, 2 * LEVELS))
                    pe.wait_ge(s("vb"), A.th(1, 1))
                    if B:
                        pe.wait_ge(s("oln"), B.th(1, 1))
                    settle(pe, s("settled_pe"))
                    for b, r in enumerate(A.blocks()):
                        for h in range(H):
                            ins = pe.matmul(bank1(4 + b)[:, h, :], kbg[r, h, :], TT[r, h, :], start=True, stop=True)
                    ins.then_inc(s("kcd"), 1)
                    for r in A.blocks():
                        for h in range(H):
                            ins = pe.matmul(bank2(0)[r, h, :], TT[r, h, :], vb[r, h, :], start=True, stop=True)
                    ins.then_inc(s("TvP"), 1)
                elif B:
                    squares_sum(B)

            stages(pe, run)

        @block.scalar
        def _(act):
            def squares_k(C):
                act.wait_ge(s("in1"), C.th(16, 16))
                act.activation(sq[:, :, 0:C.n], kk[:, :, 0:C.n], ACT.Square).then_inc(s("sqk"), 1)

            def squares_q(A):
                act.wait_ge(s("in0"), A.th(16, 16))
                act.activation(qs[:, :, 0:A.n], kq[A.odd][:, :, 0:A.n], ACT.Square, scale=EPS ** 0.5 * DK)\
                   .then_inc(s("qs"), 1)

            def decays(C):
                n = C.n
                act.wait_ge(s("clip"), C.th(1, 2))
                act.activation(low[0:n], low[0:n], ACT.Exp, scale=-1.0).then_inc(s("dlow"), 1)
                act.wait_ge(s("clip"), C.th(2, 2))
                act.activation(upi[0:n], upi[0:n], ACT.Exp).then_inc(s("dup"), 1)

            def rms(B):
                n = B.n
                act.wait_ge(s("osum"), B.th(1, 1))
                act.wait_ge(s("eps"), 1)
                act.activation(rt[:, :, 0:n], bank2(0, n), ACT.Ln, bias=m.eps[:, 1:2]).then_inc(s("oln"), 1)
                act.wait_ge(s("oln"), B.th(1, 1))
                act.activation(rt[:, :, 0:n], rt[:, :, 0:n], ACT.Exp, scale=-0.5).then_inc(s("orms"), 1)

            def run(A, B, C):
                if A:
                    n = A.n
                    act.wait_ge(s("ksum"), A.th(1, 1))
                    if not A.first:
                        act.wait_ge(s("olo"), A.th(0, 1))
                    act.activation(rt[:, :, 0:n], bank2(6, n), ACT.Ln, bias=m.eps[:, 0:1]).then_inc(s("kln"), 1)
                    act.wait_ge(s("kln"), A.th(1, 1))
                    act.activation(rt[:, :, 0:n], rt[:, :, 0:n], ACT.Exp, scale=-0.5).then_inc(s("rk"), 1)
                    act.wait_ge(s("in_eg"), A.th(32, 32) if n == P else 32 * NPAIR + 16)
                    nb = len(A.blocks())
                    act.activation(eg[:, 0:nb], eg[:, 0:nb], ACT.Exp).then_inc(s("eg"), 1)
                    act.wait_ge(s("eg"), A.th(1, 1))
                    act.copy(egl[:, A.odd, 0:nb, :], eg[:, 0:nb, :, L - 1:L].squeeze(3)).then_inc(s("egl"), 1)
                    act.wait_ge(s("vturned"), A.th(1, 1))
                    settle(act, s("settled_act"))
                    for h in range(H):
                        ins = act.mul(vb[0:n, h, :], bank2(4)[0:n, h, :],
                                      m.gcol[0:n, bass.ds(A.index, 1), H + h:H + h + 1].squeeze(1))
                    ins.then_inc(s("vb"), 1)
                if B:
                    act.wait_ge(s("o"), B.th(len(B.blocks()), 2))
                    act.activation(sq[:, :, 0:B.n], bank2(2, B.n), ACT.Square).then_inc(s("osq"), 1)
                if A:
                    for l in range(1, LEVELS):
                        for g, hs in enumerate(HALVES):
                            act.wait_ge(s("X"), A.th(2 * (l - 1) + g + 1, 2 * (LEVELS - 1)))
                            act.copy(X[0:n, hs, :], bank1(4 + g)[0:n, hs, :]).then_inc(s("Xs"), 1)
                        if l == 2:
                            if B:
                                act.wait_ge(s("osum_in"), B.th(1, 1))
                            squares_q(A)
                            if C:
                                decays(C)
                        if B and l == 3:
                            rms(B)
                    if B:
                        act.wait_ge(s("osum"), B.th(1, 1))
                    if C:
                        if not B:
                            act.wait_ge(s("ksum"), A.th(1, 1))
                        squares_k(C)
                elif B:
                    rms(B)
                if B:
                    act.wait_ge(s("ofull"), B.th(1, 1))
                    settle(act, s("settled_act"))
                    act.activation(m.xhi[:, :, bass.ds(B.col, B.n)], rt[:, :, 0:B.n], ACT.Copy).then_inc(s("ohi"), 1)
                if A:
                    act.wait_ge(s("kcd"), A.th(1, 1))
                    for b, r in enumerate(A.blocks()):
                        ins = act.copy(kc[:, :, r], bank1(4 + b))
                    ins.then_inc(s("kc"), 1)
                    act.wait_ge(s("TvP"), A.th(1, 1))
                    act.copy(kbg[0:n, :, :], bank2(0)[0:n, :, :]).then_inc(s("Tv"), 1)

            squares_k(Pair(0))
            decays(Pair(0))
            stages(act, run)

        @block.vector
        def _(dve):
            def differences(C):
                n = C.n
                dve.wait_ge(s("in_gb"), C.th(32, 32) if n == P else 32 * NPAIR + 16)
                gc = m.gcol[0:n, bass.ds(C.index, 1), 0:H].squeeze(1).unsqueeze(2).to_broadcast([n, H, L])
                dve.tensor_tensor(GB[0:n, 0], GB[0:n, 0], gc, ALU.subtract).then_inc(s("diff"), 1)
                dve.wait_ge(s("diff"), C.th(1, 1))
                dve.tensor_scalar(low[0:n], GB[0:n, 0], 0.0, None, ALU.max).then_inc(s("clip"), 1)
                dve.tensor_scalar(upi[0:n], GB[0:n, 0], 0.0, None, ALU.min).then_inc(s("clip"), 1)

            def new_values(B, b):
                r = B.blocks()[b]
                dve.wait_ge(s("Tv"), B.th(1, 1))
                for g, hs in enumerate(HALVES):
                    dve.wait_ge(s("kS"), B.th(2 * b + g + 1, 4))
                    dve.tensor_tensor(vn[r, hs, :], kbg[r, hs, :], bank2(0)[r, hs, :], ALU.subtract)\
                       .then_inc(s("vn"), 1)

            def state_add(B, b):
                dve.wait_ge(s("dS"), B.th(b + 1, 2))
                dve.wait_ge(s("Sg"), B.th(b + 1, 2))
                dve.tensor_tensor(S[1 - b][:, :, :], bank2(4), Sg[:, :, :], ALU.add).then_inc(s("S"), 1)

            def normed(B):
                n = B.n
                dve.wait_ge(s("orms"), B.th(1, 1))
                dve.scalar_tensor_tensor(rt[:, :, 0:n], bank2(2, n), m.go[:, 0:1], rt[:, :, 0:n], ALU.mult, ALU.mult)\
                   .then_inc(s("onorm"), 1)

            def run(A, B, C):
                if A:
                    n = A.n
                    dve.wait_ge(s("rk"), A.th(1, 1))
                    dve.tensor_tensor(kk[:, :, 0:n], kk[:, :, 0:n], rt[:, :, 0:n], ALU.mult).then_inc(s("kn"), 1)
                if B:
                    new_values(B, 0)
                if A:
                    dve.wait_ge(s("gramk"), A.th(1, 1))
                    dve.wait_ge(s("low_b"), A.th(1, 1))
                    dve.tensor_tensor(T[0:n], bank1(6)[0:n], low[0:n], ALU.mult).then_inc(s("Ta"), 1)
                    dve.wait_ge(s("upl"), A.th(1, 1))
                    dve.tensor_tensor(TT[0:n], bank1(6)[0:n], upl[0:n], ALU.mult).then_inc(s("Ta"), 1)
                    dve.tensor_tensor(MT[0:n], bank1(6)[0:n], ups[0:n], ALU.mult).then_inc(s("MT"), 1)
                if B:
                    state_add(B, 0)
                if A:
                    dve.wait_ge(s("Ta"), A.th(2, 2))
                    dve.tensor_tensor(TT[0:n], TT[0:n], masked(m.EYE, n), ALU.add).then_inc(s("TT0"), 1)
                    dve.tensor_tensor(T[0:n], T[0:n], masked(m.EYE, n), ALU.add).then_inc(s("T0"), 1)
                    dve.wait_ge(s("gramq"), A.th(1, 1))
                    dve.wait_ge(s("upi_m"), A.th(1, 1))
                    dve.tensor_tensor(AT[A.odd][0:n], bank1(7)[0:n], upi[0:n], ALU.mult).then_inc(s("AT"), 1)
                if B and B.n == P:
                    new_values(B, 1)
                if A:
                    dve.wait_ge(s("kturned"), A.th(1, 1))
                    if B:
                        dve.wait_ge(s("vn"), B.th(4, 4) if B.n == P else B.th(2, 4))
                    dve.tensor_tensor(kbg[0:n], bank2(6)[0:n],
                                      m.bcol[0:n, bass.ds(A.index, 1), :].squeeze(1).unsqueeze(2).to_broadcast([n, H, P]),
                                      ALU.mult)
                    dve.tensor_tensor(ktl[A.odd][0:n], bank2(6)[0:n],
                                      upi[0:n, :, L - 1:L].to_broadcast([n, H, P]), ALU.mult).then_inc(s("kscaled"), 1)
                    dve.wait_ge(s("T0"), A.th(1, 1))
                    dve.wait_ge(s("TT0"), A.th(1, 1))
                    for g in range(2):
                        dve.sem_inc(s("T"), 1)
                        dve.sem_inc(s("TT"), 1)
                if B and B.n == P:
                    state_add(B, 1)
                if A:
                    for l in range(1, LEVELS):
                        for g, hs in enumerate(HALVES):
                            y = bank1(6 + g)[0:n]
                            dve.wait_ge(s("Y"), A.th(2 * (l - 1) + g + 1, 2 * (LEVELS - 1)))
                            if l < LEVELS - 1:
                                dve.tensor_tensor(T[0:n, hs], T[0:n, hs], y[:, 0:GR], ALU.subtract).then_inc(s("T"), 1)
                            dve.tensor_tensor(TT[0:n, hs], TT[0:n, hs], y[:, GR:H], ALU.subtract).then_inc(s("TT"), 1)
                        if l == 1 and C:
                            dve.wait_ge(s("kscaled"), A.th(1, 1))
                            dve.wait_ge(s("AT"), A.th(1, 1))
                            differences(C)
                        if B and l == 3:
                            normed(B)
                elif B:
                    normed(B)

            dve.memset(m.xhi[:, :, SEQ:S0].bitcast(F32), 0.0)
            dve.memset(m.xlo[:, :, SEQ:S0].bitcast(F32), 0.0)
            differences(Pair(0))
            stages(dve, run)



def build(nc, d):
    with ExitStack() as ctx:
        m = Box()
        m.limbo = []
        sb = lambda c, n, shape, dt=F32: c.enter_context(nc.sbuf_tensor(n, shape, dt))
        m.ident = sb(ctx, "ident", [P, P])
        m.ones = sb(ctx, "ones", [P, P])
        m.eps = sb(ctx, "eps", [P, 8])
        m.par = sb(ctx, "par", [P, 6 * P])
        m.alog = sb(ctx, "alog", [HEADS, 8])[:, 0:1]
        m.dtb = sb(ctx, "dtb", [HEADS, 8])[:, 0:1]
        m.strow = sb(ctx, "strow", [P, P])
        m.EYE, m.UPI, m.UPS, m.LEV, m.LEVT = range(5)
        with ExitStack() as c:
            m.wraw = sb(c, "wraw", [P, RAW, UNIT])
            m.whi = sb(c, "whi", [P, 4, UNIT], F32R)
            m.wlo = sb(c, "wlo", [P, 4, UNIT], F32R)
        with ExitStack() as c:
            m.delta_small = [sb(c, "dn_ML", [P, LEVELS - 1, HEADS, CH])]
            m.delta_small += [sb(c, "dn_" + n, [P, HEADS, CH])
                              for n in ("T", "TT", "X", "MT", "AT0", "AT1", "low", "upi", "ups", "upl")]
        sb(ctx, "w_place", [P, RAW + 8, UNIT])
        m.ps = ctx.enter_context(nc.psum_tensor("ps", [P, 8, 512], F32))
        with ExitStack() as c:
            m.xhi = sb(c, "xhi", [P, KD, TW], F32R)
            m.xlo = sb(c, "xlo", [P, KD, TW], F32R)
        with ExitStack() as c:
            m.qT = sb(c, "qT", [P, KD, TW])
            m.kT = sb(c, "kT", [P, KD, TW])
        with ExitStack() as c:
            sb(c, "q_place", [P, KD, TW])
            m.qhi = sb(c, "qhi", [P, KQ, TW], F32R)
            m.qlo = sb(c, "qlo", [P, KQ, TW], F32R)
        sb(ctx, "x_place", [P, 2 * KD, TW])

        with ExitStack() as c:
            m.z = sb(c, "z", [P, KD, TW])
            inputs_block(nc, ctx, m, d)
        with ExitStack() as c:
            m.osc = sb(c, "osc", [P, SC // P, TW])
            with ExitStack() as cc:
                m.ckv = sb(cc, "ckv", [P, KKV, TW])
                m.krf = sb(cc, "krf", [P, TW])
                with ExitStack() as c3:
                    m.cq = sb(c3, "cq", [P, KQ, TW])
                    even_in_block(nc, ctx, m, d)
                    queries_block(nc, ctx, m, d)
                m.V = sb(cc, "V", [P, NTOK + 3, HEADS * V_DIM])
                m.kpast = sb(cc, "kpast", [P, HEADS, PAST])
                keys_block(nc, ctx, m, d)
                attention_block(nc, ctx, m, d)
        with ExitStack() as c:
            m.z = sb(c, "z2", [P, KD, TW])
            out_block(nc, ctx, m, d, "eo", d["w_o_e"][0], [2 * k + 1 for k in range(4)] + [2 * k for k in range(4)])
            layer_norm_block(nc, ctx, m, d, "ln0", 0, "mix", "ffn")
            ffn_block(nc, ctx, m, d, 0)
            layer_norm_block(nc, ctx, m, d, "ln1", 0, "ff", "mixer")
        with ExitStack() as c:
            m.gcol = sb(c, "gcol", [P, 9, 16])
            m.bcol = sb(c, "bcol", [P, 9, HEADS])
            m.go = sb(c, "go", [P, 8])
            m.masks = sb(c, "masks", [P, 5, CH])
            m.levt = sb(c, "levt", [P, LEVELS - 1, CH])
            with ExitStack() as cc:
                m.G = sb(cc, "G", [HEADS, TW])
                m.beta = sb(cc, "beta", [HEADS, TW])
                m.ab = sb(cc, "ab", [2 * HEADS, TW])
                m.bt = sb(cc, "bt", [HEADS, TW])
                odd_in_block(nc, ctx, m, d)
                gates_block(nc, ctx, m, d)
            delta_block(nc, ctx, m, d)
        with ExitStack() as c:
            m.z = sb(c, "z3", [P, KD, TW])
            out_block(nc, ctx, m, d, "oo", d["w_o_o"][0], range(KD))
            layer_norm_block(nc, ctx, m, d, "ln2", 1, "mix", "ffn")
            ffn_block(nc, ctx, m, d, 1)
            layer_norm_block(nc, ctx, m, d, "ln3", 1, "ff", "out")


_INS = ["x_prompt", "x_sample", "cache_mla_latent", "cache_mla_krope", "state_sconv", "state_dconv",
        "state_delta", "state_ffconv", "w_in_e", "g_qnorm", "g_kvnorm", "w_uq", "w_ukv", "sc_w", "w_o_e",
        "w_in_o", "dconv_w", "a_log", "dt_bias", "g_onorm", "w_o_o", "w_ff_in", "ffconv_w", "w_ff_out",
        "ln_mix_g", "ln_mix_b", "ln_ff_g", "ln_ff_b"]
_OUTS = [("y_p", (1, SEQ, D)), ("y_s", (1, DEC, D)), ("p_latent", (1, 1, SEQ, KV_RANK)),
         ("p_krope", (1, 1, SEQ, ROPE)), ("p_sconv", (1, 1, 2, SC)), ("p_dconv", (1, 1, 3, 3 * DN_KEY)),
         ("p_delta", (1, 1, HEADS, DK, DK)), ("p_ffconv", (2, 1, 2, F)),
         ("s_latent", (1, 1, DEC, KV_RANK)), ("s_krope", (1, 1, DEC, ROPE)), ("s_sconv", (1, 1, 2, SC)),
         ("s_dconv", (1, 1, 3, 3 * DN_KEY)), ("s_delta", (1, 1, HEADS, DK, DK)), ("s_ffconv", (2, 1, 2, F))]


def kernel(**inputs):
    import numpy as np
    import concourse.bacc as bacc
    from concourse.bass_utils import run_bass_kernel_spmd

    nc = bacc.Bacc("TRN2", target_bir_lowering=False, num_devices=1)
    half = ROPE // 2
    inv = np.power(np.float32(10000.0), -np.arange(half, dtype=np.float32) / np.float32(half))
    pos = np.concatenate([np.arange(SEQ), np.zeros(GAP), PAST + np.arange(DEC)]).astype(np.float32)
    ang = (pos[None, :] * inv[:, None]).astype(np.float32)
    tables = {"rope_cos": np.concatenate([np.cos(ang), np.cos(ang)]).astype(np.float32),
              "rope_sin": np.concatenate([-np.sin(ang), np.sin(ang)]).astype(np.float32)}
    arrays, d = {}, {}
    for name in _INS + list(tables):
        a = np.ascontiguousarray(tables[name] if name in tables else inputs[name])
        arrays[f"in_{name}"] = a
        d[name] = nc.dram_tensor(f"in_{name}", a.shape, mybir.dt.from_np(a.dtype), kind="ExternalInput").ap()
    for i, (name, shape) in enumerate(_OUTS):
        d[name] = nc.dram_tensor(f"out_{i}", shape, F32, kind="ExternalOutput").ap()
    d["residual"] = nc.dram_tensor("residual", (P, KD * TW), F32, kind="Internal").ap()
    d["qkvz"] = nc.dram_tensor("qkvz", (4, HEADS, P, TW), F32, kind="Internal").ap()
    d["gates"] = nc.dram_tensor("gates", (NCHUNK, 2, HEADS, CH), F32, kind="Internal").ap()
    build(nc, d)
    r = run_bass_kernel_spmd(nc, [arrays], core_ids=[0])
    return tuple(r.results[0][f"out_{i}"] for i in range(len(_OUTS)))
```
